# Optimizing a Trainium2 kernel written in Bass

```python
import jax, jax.numpy as jnp
from jax import lax
import numpy as np

D_MODEL = 1024
BATCH = 1
SEQ = 256
DEPTH = 2
DEC_BATCH = 8
DEC_SEQ = 4
PAST_LEN = 2048
PAGE_SIZE = 128

N_MIXERS = 2
N_CONV = (DEPTH + 1) // 2
N_RWKV = DEPTH // 2
CONV_WIDTH = 3
HEAD_SIZE = 64
N_HEADS = D_MODEL // HEAD_SIZE
D_DECAY_LORA = 64
D_AAA_LORA = 64
D_MV_LORA = 32
D_GATE_LORA = 128
N_KEYS = 128
N_EXPERTS = N_KEYS * N_KEYS
PEER_HEADS = 8
PEER_TOPK = 16
D_QUERY = 256
PEER_CHUNK = 256
RMS_EPS = 1e-6
GN_EPS = 64e-5

kernel_name = "hybrid_conv_rwkv7_peer_adaln_step"

def rmsnorm(x, g):
    x32 = x.astype(jnp.float32)
    y = x32 * lax.rsqrt(jnp.mean(x32 * x32, axis=-1, keepdims=True) + RMS_EPS)
    return y.astype(x.dtype) * g

def modulate(h, shift, scale):
    return h * (1 + scale[:, None, :]) + shift[:, None, :]

def conv_mixer(h, prev, w_in, conv_k, w_out):
    T = h.shape[1]
    bg, cg, xp = jnp.split(h @ w_in, 3, axis=-1)
    u = cg * xp
    up = jnp.concatenate([prev.astype(u.dtype), u], axis=1)
    conv = up[:, 0:T] * conv_k[0]
    for j in range(1, CONV_WIDTH):
        conv = conv + up[:, j:j + T] * conv_k[j]
    y = (bg * conv) @ w_out
    return y, up[:, -(CONV_WIDTH - 1):]

def wkv_scan(r, w, k, v, a, b, s0):
    def step(S, inp):
        rt, wt, kt, vt, at, bt = inp
        sa = jnp.einsum('bhij,bhj->bhi', S, at)
        S = S * wt[:, :, None, :] + sa[..., None] * bt[:, :, None, :] + vt[..., None] * kt[:, :, None, :]
        return S, jnp.einsum('bhij,bhj->bhi', S, rt)
    xs = tuple(jnp.moveaxis(t, 1, 0) for t in (r, w, k, v, a, b))
    S, ys = lax.scan(step, s0, xs)
    return jnp.moveaxis(ys, 0, 1), S

def rwkv_mixer(h, prev, s0, mix, wr, wk, wv, wo, w0, w1, w2, a0, a1, a2, g1, g2,
               k_k, k_a, r_k, lnw, lnb, v_first, vres):
    B, T, D = h.shape
    hs = jnp.concatenate([prev[:, None, :].astype(h.dtype), h[:, :-1]], axis=1)
    xx = hs - h
    xr, xw, xk, xv, xa, xg = [h + xx * mix[i] for i in range(6)]
    r = xr @ wr
    wlog = -jax.nn.softplus(-(w0 + jnp.tanh(xw @ w1) @ w2)) - 0.5
    k = xk @ wk
    v = xv @ wv
    if vres is None:
        v_first = v
    else:
        v0, v1, v2 = vres
        v = v + (v_first - v) * jax.nn.sigmoid(v0 + (xv @ v1) @ v2)
    a = jax.nn.sigmoid(a0 + (xa @ a1) @ a2)
    g = jax.nn.sigmoid(xg @ g1) @ g2
    heads = lambda t: t.reshape(B, T, N_HEADS, HEAD_SIZE).astype(jnp.float32)
    kk = heads(k * k_k)
    kk = kk * lax.rsqrt(jnp.maximum(jnp.sum(kk * kk, axis=-1, keepdims=True), 1e-24))
    k = k * (1 + (a - 1) * k_a)
    r_h, k_h, v_h, a_h = heads(r), heads(k), heads(v), heads(a)
    decay = jnp.exp(-jnp.exp(heads(wlog)))
    y, S = wkv_scan(r_h, decay, k_h, v_h, -kk, kk * a_h, s0.astype(jnp.float32))
    mu = jnp.mean(y, axis=-1, keepdims=True)
    var = jnp.mean(jnp.square(y - mu), axis=-1, keepdims=True)
    y = ((y - mu) * lax.rsqrt(var + GN_EPS)).reshape(B, T, D) * lnw + lnb
    bonus = jnp.sum(r_h * k_h * r_k, axis=-1, keepdims=True) * v_h
    y = y + bonus.reshape(B, T, D)
    out = (y.astype(h.dtype) * g) @ wo
    return out, h[:, -1], S, v_first

def peer_ffn(h, wq, k1, k2, u_tab, v_tab):
    B, T, D = h.shape
    n = B * T
    n_pad = -(-n // PEER_CHUNK) * PEER_CHUNK
    flat = jnp.pad(h.reshape(n, D), ((0, n_pad - n), (0, 0)))
    half = D_QUERY // 2

    def chunk(hc):
        q = (hc @ wq).reshape(-1, PEER_HEADS, D_QUERY)
        s1 = jnp.einsum('chd,hkd->chk', q[..., :half], k1).astype(jnp.float32)
        s2 = jnp.einsum('chd,hkd->chk', q[..., half:], k2).astype(jnp.float32)
        v1, i1 = lax.top_k(s1, PEER_TOPK)
        v2, i2 = lax.top_k(s2, PEER_TOPK)
        cand = (v1[..., :, None] + v2[..., None, :]).reshape(-1, PEER_HEADS, PEER_TOPK * PEER_TOPK)
        sc, ci = lax.top_k(cand, PEER_TOPK)
        e1 = jnp.take_along_axis(i1, ci // PEER_TOPK, axis=-1)
        e2 = jnp.take_along_axis(i2, ci % PEER_TOPK, axis=-1)
        eidx = e1 * N_KEYS + e2
        gate = jax.nn.softmax(sc, axis=-1)
        z = jax.nn.gelu(jnp.einsum('cd,chkd->chk', hc, u_tab[eidx]), approximate=False)
        coef = (gate * z.astype(jnp.float32)).astype(hc.dtype)
        return jnp.einsum('chk,chkd->cd', coef, v_tab[eidx])

    out = lax.map(chunk, flat.reshape(-1, PEER_CHUNK, D))
    return out.reshape(n_pad, D)[:n].reshape(B, T, D)

def setup_inputs(seed: int = 0) -> dict:
    key = jax.random.key(seed)
    ks = iter(jax.random.split(key, 48))
    D = D_MODEL
    inv = D ** -0.5
    nrm = lambda shape, s: jax.random.normal(next(ks), shape, jnp.float32) * s
    uni = lambda shape, lo, hi: jax.random.uniform(next(ks), shape, jnp.float32, lo, hi)
    return {
        "x_prompt": nrm((BATCH, SEQ, D), 1.0),
        "x_sample": nrm((DEC_BATCH, DEC_SEQ, D), 1.0),
        "state_conv": nrm((N_CONV, DEC_BATCH, CONV_WIDTH - 1, D), 0.5),
        "state_shift": nrm((N_RWKV, DEC_BATCH, D), 1.0),
        "state_wkv": nrm((N_RWKV, DEC_BATCH, N_HEADS, HEAD_SIZE, HEAD_SIZE), 0.1),
        "c_prompt": nrm((BATCH, D), 1.0),
        "c_sample": nrm((DEC_BATCH, D), 1.0),
        "w_ada": nrm((DEPTH, D, 6 * D), 0.5 * inv),
        "b_ada": nrm((DEPTH, 6 * D), 0.02),
        "g_mix": 1.0 + nrm((DEPTH, D), 0.02),
        "g_ffn": 1.0 + nrm((DEPTH, D), 0.02),
        "g_final": 1.0 + nrm((D,), 0.02),
        "conv_w_in": nrm((N_CONV, D, 3 * D), inv),
        "conv_k": nrm((N_CONV, CONV_WIDTH, D), CONV_WIDTH ** -0.5),
        "conv_w_out": nrm((N_CONV, D, D), inv),
        "rwkv_mix": uni((N_RWKV, 6, D), 0.0, 1.0),
        "rwkv_wr": nrm((N_RWKV, D, D), inv),
        "rwkv_wk": nrm((N_RWKV, D, D), inv),
        "rwkv_wv": nrm((N_RWKV, D, D), inv),
        "rwkv_wo": nrm((N_RWKV, D, D), inv),
        "rwkv_w0": uni((N_RWKV, D), -6.0, 1.0),
        "rwkv_w1": nrm((N_RWKV, D, D_DECAY_LORA), inv),
        "rwkv_w2": nrm((N_RWKV, D_DECAY_LORA, D), 0.5 * D_DECAY_LORA ** -0.5),
        "rwkv_a0": nrm((N_RWKV, D), 0.1),
        "rwkv_a1": nrm((N_RWKV, D, D_AAA_LORA), inv),
        "rwkv_a2": nrm((N_RWKV, D_AAA_LORA, D), 0.5 * D_AAA_LORA ** -0.5),
        "rwkv_v0": nrm((N_RWKV - 1, D), 0.1),
        "rwkv_v1": nrm((N_RWKV - 1, D, D_MV_LORA), inv),
        "rwkv_v2": nrm((N_RWKV - 1, D_MV_LORA, D), 0.5 * D_MV_LORA ** -0.5),
        "rwkv_g1": nrm((N_RWKV, D, D_GATE_LORA), inv),
        "rwkv_g2": nrm((N_RWKV, D_GATE_LORA, D), D_GATE_LORA ** -0.5),
        "rwkv_k_k": 0.85 + nrm((N_RWKV, D), 0.02),
        "rwkv_k_a": 1.0 + nrm((N_RWKV, D), 0.02),
        "rwkv_r_k": nrm((N_RWKV, N_HEADS, HEAD_SIZE), 0.1),
        "rwkv_lnw": 1.0 + nrm((N_RWKV, D), 0.02),
        "rwkv_lnb": nrm((N_RWKV, D), 0.02),
        "peer_wq": nrm((DEPTH, D, PEER_HEADS * D_QUERY), inv),
        "peer_k1": nrm((DEPTH, PEER_HEADS, N_KEYS, D_QUERY // 2), (D_QUERY // 2) ** -0.5),
        "peer_k2": nrm((DEPTH, PEER_HEADS, N_KEYS, D_QUERY // 2), (D_QUERY // 2) ** -0.5),
        "peer_u": nrm((DEPTH, N_EXPERTS, D), inv),
        "peer_v": nrm((DEPTH, N_EXPERTS, D), 0.5),
    }

def reference(x_prompt, x_sample, state_conv, state_shift, state_wkv, c_prompt, c_sample,
              w_ada, b_ada, g_mix, g_ffn, g_final, conv_w_in, conv_k, conv_w_out,
              rwkv_mix, rwkv_wr, rwkv_wk, rwkv_wv, rwkv_wo, rwkv_w0, rwkv_w1, rwkv_w2,
              rwkv_a0, rwkv_a1, rwkv_a2, rwkv_v0, rwkv_v1, rwkv_v2, rwkv_g1, rwkv_g2,
              rwkv_k_k, rwkv_k_a, rwkv_r_k, rwkv_lnw, rwkv_lnb,
              peer_wq, peer_k1, peer_k2, peer_u, peer_v):
    def run(x, c, st_conv, st_shift, st_wkv):
        cs = jax.nn.silu(c)
        new_conv, new_shift, new_wkv = [], [], []
        v_first = None
        for i in range(DEPTH):
            m = cs @ w_ada[i] + b_ada[i]
            sh_m, sc_m, gt_m, sh_f, sc_f, gt_f = jnp.split(m, 6, axis=-1)
            h = modulate(rmsnorm(x, g_mix[i]), sh_m, sc_m)
            j = i // N_MIXERS
            if i % N_MIXERS == 0:
                y, cbuf = conv_mixer(h, st_conv[j], conv_w_in[j], conv_k[j], conv_w_out[j])
                new_conv.append(cbuf)
            else:
                vres = None if j == 0 else (rwkv_v0[j - 1], rwkv_v1[j - 1], rwkv_v2[j - 1])
                y, last, S, v_first = rwkv_mixer(
                    h, st_shift[j], st_wkv[j], rwkv_mix[j], rwkv_wr[j], rwkv_wk[j], rwkv_wv[j], rwkv_wo[j],
                    rwkv_w0[j], rwkv_w1[j], rwkv_w2[j], rwkv_a0[j], rwkv_a1[j], rwkv_a2[j],
                    rwkv_g1[j], rwkv_g2[j], rwkv_k_k[j], rwkv_k_a[j], rwkv_r_k[j],
                    rwkv_lnw[j], rwkv_lnb[j], v_first, vres)
                new_shift.append(last)
                new_wkv.append(S)
            x = x + gt_m[:, None, :] * y
            h = modulate(rmsnorm(x, g_ffn[i]), sh_f, sc_f)
            x = x + gt_f[:, None, :] * peer_ffn(h, peer_wq[i], peer_k1[i], peer_k2[i], peer_u[i], peer_v[i])
        return rmsnorm(x, g_final), jnp.stack(new_conv), jnp.stack(new_shift), jnp.stack(new_wkv)

    D = D_MODEL
    p_conv0 = jnp.zeros((N_CONV, BATCH, CONV_WIDTH - 1, D), x_prompt.dtype)
    p_shift0 = jnp.zeros((N_RWKV, BATCH, D), x_prompt.dtype)
    p_wkv0 = jnp.zeros((N_RWKV, BATCH, N_HEADS, HEAD_SIZE, HEAD_SIZE), jnp.float32)
    y_prompt, p_conv, p_shift, p_wkv = run(x_prompt, c_prompt, p_conv0, p_shift0, p_wkv0)
    y_sample, s_conv, s_shift, s_wkv = run(x_sample, c_sample, state_conv, state_shift, state_wkv)
    return (y_prompt, y_sample, p_conv, p_shift, p_wkv, s_conv, s_shift, s_wkv)


_drawn_inputs = setup_inputs


def setup_inputs(seed=0):
    import zlib

    import numpy as np

    out = dict(_drawn_inputs(seed))
    spreads = {}
    factors = {'g_ffn': 3.232, 'g_final': 2.838, 'rwkv_lnw': 8.0, 'rwkv_lnb': 8.0}
    for name, (base, spread) in spreads.items():
        noise = np.random.default_rng([zlib.crc32(name.encode()), seed]).standard_normal(out[name].shape)
        drawn = base * np.exp(spread * noise) if base else spread * noise
        out[name] = __import__('jax').numpy.asarray(drawn.astype(out[name].dtype))
    for name, factor in factors.items():
        out[name] = (out[name] * factor).astype(out[name].dtype)
    return out
```

```python
from contextlib import ExitStack

import numpy as np
import concourse.bass as bass
from concourse import mybir

ALU = mybir.AluOpType
ACT = mybir.ActivationFunctionType
F32 = mybir.dt.float32
U32 = mybir.dt.uint32
AX_X = mybir.AxisListType.X

P = 128
D = 1024
DC = D // P
NP_TOK = 256
NSEQ, NSTEP = 8, 4
NS_TOK = NSEQ * NSTEP
TOK = NP_TOK + NS_TOK
NCOND = 1 + NSEQ
DEPTH = 2
EPS = 1e-6
HEADS = 8
NKEYS = 128
NEXP = NKEYS * NKEYS
TOPK = 16
UNITS = 18
RING = 8
NDIAG = 4
WRING = 4
BANKS = 4
NEG = -3.0e38
NSEL = 29
SEL_IDX = 26
GN_EPS = 64e-5
WHEADS, HS = 16, 64
DECAY = -float(np.exp(-0.5))
CHUNK = 64
NQ = NP_TOK // CHUNK
LW_, LA_, LG_ = 64, 64, 128

ROWS = {}


def _rows():
    at = 0
    for name, n in (("g_mix", 16), ("g_ffn", 16), ("g_final", 8), ("conv_k", 24), ("rwkv_mix", 48),
                    ("rwkv_w0", 8), ("rwkv_a0", 8), ("rwkv_k_k", 8), ("rwkv_k_a", 8), ("rwkv_r_k", 8),
                    ("rwkv_lnw", 8), ("rwkv_lnb", 8), ("b_ada0", 48), ("pad", 40), ("b_ada1", 48)):
        ROWS[name] = at
        at += n
    return at


NROWS = _rows()
PAR_ROWS = (P, ROWS["b_ada0"] + 48 - P, 48)
CR_COND, CR_CONV, CR_SHIFT, CR_N = 0, NCOND, NCOND + 2 * NSEQ, NCOND + 3 * NSEQ

STAGES = [("par", 1), ("crow", 1), ("x", DC), ("ada", 2 * 16), ("nrm0", 1), ("cin", 24), ("cout", DC), ("cst", 2)]
STAGES += [("nrm1", 1), ("kt0", 4), ("q0", 16), ("sc0", 9), ("ht0", 6), ("res0", DC)]
STAGES += [("nrm2", 1), ("sst", 2), ("rp", DC), ("kp", DC), ("vp", DC), ("lm", 3), ("l2", 24), ("kn", DC), ("bn", DC), ("adb", 2 * 8)]
NM_STEPS, NM_STEPS_S = 21, 7
for _t in range(2):
    STAGES += [(f"tm{_t}", 6), (f"nm{_t}", 4 * NM_STEPS), (f"sq{_t}", 16)] + [("pso", 2)] * (_t == 1) + [(f"gn{_t}", 2)]
STAGES += [("tm2", 6), ("nm2", 4 * NM_STEPS_S), ("sq2", 9 * DC), ("gn2", 2), ("wo", DC)]
STAGES += [("nrm3", 1), ("kt1", 4), ("q1", 16), ("sc1", 9), ("ht1", 6), ("res1", DC)]
STAGES += [("nrm4", 1), ("fin", 6)]

SQ2 = []
for _c in range(-1, DC + 1):
    SQ2 += [("turn0", _c + 1), ("turn1", _c + 1), ("sa", _c), ("out0", _c - 1), ("out1", _c - 1),
            ("right", _c + 1), ("y", _c), ("new0", _c), ("new1", _c)]
SQ2 = [g for g in SQ2 if 0 <= g[1] < DC]
GROUP = {}
_n = 0
for _name, _count in STAGES:
    GROUP[_name] = _n
    _n += _count


class Steps:

    def __init__(self, eng, sem):
        self.eng, self.sem, self.counts, self.last = eng, sem, {}, None

    def do(self, ins, sem=None):
        sem = sem or self.sem
        ins.then_inc(sem, 1)
        self.counts[sem.name] = self.counts.get(sem.name, 0) + 1
        self.last = (sem, self.counts[sem.name])
        return ins

    def sync(self):
        if self.last:
            self.eng.wait_ge(*self.last)

    def chain(self, ins, sem=None):
        self.do(ins, sem)
        self.sync()


def build(nc, a, out):
    with ExitStack() as ctx:
        def sb(name, shape, dt=F32):
            return ctx.enter_context(nc.sbuf_tensor(name, [P] + list(shape), dt))

        def sem(name):
            return ctx.enter_context(nc.semaphore(name))

        ps = ctx.enter_context(nc.psum_tensor("ps", [P, 8, 512], F32))
        X = sb("X", [DC, TOK])
        H = sb("H", [DC, TOK])
        PAR = sb("PAR", [3 * P])
        CT = sb("CT", [DC, CR_N])
        ADA = sb("ADA", [DEPTH, 48, NCOND])
        GA = sb("GA", [2 * DEPTH, DC, NCOND])
        ident = sb("ident", [P])
        ones = sb("ones", [P])
        sel = sb("sel", [NS_TOK])
        iota16 = sb("iota16", [TOPK])
        rms = sb("rms", [TOK])
        rstd = sb("rstd", [TOK])
        tmpS = sb("tmpS", [2, NS_TOK])
        W = sb("W", [WRING, DC, 512])
        N_RV, N_ROWS, N_SEL = 2 * RING * D, 3 * D, 2880
        ARENA = sb("ARENA", [N_RV + 2 * N_ROWS + N_SEL])
        RV = ARENA[:, 0:N_RV]
        HTOK = ARENA[:, N_RV:N_RV + N_ROWS].rearrange("p (a d) -> p a d", a=3)
        OACC = ARENA[:, N_RV + N_ROWS:N_RV + 2 * N_ROWS].rearrange("p (a d) -> p a d", a=3)
        CURU = sb("CURU", [2, TOPK], U32)
        CURV = sb("CURV", [2, TOPK], U32)
        ZB = sb("ZB", [2, TOPK])
        GL = sb("GL", [2, TOPK])
        CF = sb("CF", [2, TOPK])
        DG = sb("DG", [NDIAG, P])
        scr = sb("scr", [2, 256])
        gsm = sb("gsm", [2, 2])
        COUT = sb("COUT", [DC, 18])

        rings = RV.rearrange("p (r s d) -> p r s d", r=2, s=RING)
        RU, RVV = rings[:, 0], rings[:, 1]

        def carve(off, shape, dt=F32):
            n = int(np.prod(shape))
            v = ARENA[:, off:off + n]
            if dt is not F32:
                v = v.bitcast(dt)
            names = " ".join("abcd"[:len(shape)])
            return v.rearrange(f"p ({names}) -> p {names}", **{"abcd"[i]: s for i, s in enumerate(shape)})

        PR = carve(0, [3, P])
        XR = carve(384, [3, D])
        CRAW = carve(384 + 3 * D, [D])
        SQ = carve(0, [DC, TOK])
        HN = carve(DC * TOK, [DC, TOK])
        BG = carve(0, [DC, TOK])
        CG = carve(DC * TOK, [DC, TOK])
        UHW = NP_TOK + 2 + NSEQ * 6
        UH = carve(2 * DC * TOK, [DC, UHW])
        CV = carve(2 * DC * TOK + DC * UHW, [DC, TOK])
        CS = carve(2 * DC * TOK + DC * UHW + DC * TOK, [2, DC * NS_TOK])
        CROW = carve(N_RV + N_ROWS, [D])
        KR = carve(0, [2, HEADS, P])
        KT = carve(2048, [2, HEADS, NKEYS])
        Q = carve(4096, [16, TOK])
        QP = carve(8704, [16, P])
        HS4 = carve(15360, [DC, P])
        CROW2 = carve(11 * DC * TOK - D, [D])
        YT = carve(2 * DC * TOK, [3, D])

        sel0 = N_RV + 2 * N_ROWS
        SCUR = carve(sel0, [2, 2, NKEYS])
        CAND = carve(sel0 + 512, [256])
        REST = carve(sel0 + 768, [2, 256])
        ONEHOT = carve(sel0 + 1280, [2, 256])
        sm = carve(sel0 + 1792, [16, TOPK])
        VAL, KEY, BEST, AT = sm[:, 0:2], sm[:, 2:4].bitcast(U32), sm[:, 4], sm[:, 5].bitcast(U32)
        POS = sm[:, 6:8].bitcast(U32)
        KEYF, IDX, GATE = sm[:, 8:10], sm[:, 10:12], sm[:, 12:14]
        SCALL = W[:].rearrange("p s c m -> p (s c m)")[:, 8192:8192 + UNITS * 256].rearrange("p (u n) -> p u n", u=UNITS)
        ADR = (scr[:].rearrange("p a b -> p (a b)"), DG[:].rearrange("p a b -> p (a b)"))

        FM = DC * TOK
        RF, KF, VF, BF, AF, GF, BON, LW, XX, XI0, XI1 = (carve(i * FM, [DC, TOK]) for i in range(11))
        rest = 7 * FM
        VT, BT, KTK = (carve(rest + i * D, [D]) for i in range(3))
        YR = carve(rest + 3 * D, [D])
        SB = carve(rest + 4 * D, [DC, P])
        RH = carve(rest + 5 * D, [DC, P])
        SA = carve(rest + 6 * D, [DC, P])
        RAW = carve(rest + 7 * D, [2, NSEQ, P])
        OUTB = carve(rest + 5 * D, [2, NSEQ, P])
        PSO = carve(rest + 5 * D, [DC, P])
        Wf = W[:].rearrange("p s c m -> p (s c m)")
        NT = Wf[:, 0:8192].rearrange("p (b k h t) -> p b k h t", b=2, k=8, h=4)
        GG = Wf[:, 8192:16384].rearrange("p (i h t) -> p i h t", i=4, h=WHEADS)
        gs = Wf[:, 8192:16384]
        GKV = gs[:, 0:1024].rearrange("p (h r t) -> p h r t", h=WHEADS, r=2)
        G13 = gs[:, 1024:2048].rearrange("p (r h t) -> p r h t", r=2, h=WHEADS)
        GS = (GKV[:, :, 0], G13[:, 0], GKV[:, :, 1], G13[:, 1])
        SS = gs[:, 2048:4096].rearrange("p (e s n) -> p e s n", e=2, s=NSEQ)
        NEW = gs[:, 4096:6144].rearrange("p (e s n) -> p e s n", e=2, s=NSEQ)
        ART = gs[:, 6144:7168].rearrange("p (e s r t) -> p e s r t", e=2, s=NSEQ, r=2)
        RHS = gs[:, 7168:7168 + P]
        SAV = KTK
        SAVM = SB.rearrange("p c n -> p (c n)").rearrange("p (s n) -> p s n", s=NSEQ)
        L1 = W[:, 2].rearrange("p c m -> p (c m)")[:, 0:2048].rearrange("p (c m) -> p c m", c=DC)
        L2 = W[:, 3].rearrange("p c m -> p (c m)")[:, 0:3072].rearrange("p (c m) -> p c m", c=3)
        LM = W[:, 3].rearrange("p c m -> p (c m)")[:, 3072:3072 + 3 * TOK].rearrange("p (c m) -> p c m", c=3)
        MASKS = sb("MASKS", [8, P])
        M8U, M8A, O8A, O16A, O32A, S64U, I64U, BLK = (MASKS[:, i] for i in range(8))
        MS = sb("MS", [3, NS_TOK])
        M4U, M4A, I4U = (MS[:, i] for i in range(3))
        SEQM = sb("SEQM", [NSEQ, NS_TOK])
        TOKM = sb("TOKM", [NSEQ])
        SCM = sb("SCM", [TOK])
        FE = sb("FE", [DC, NQ])
        EC = sb("EC", [DC, NSEQ])
        BBS = sb("BBS", [2, DC, NS_TOK])
        OMKA = sb("OMKA", [DC])
        gst = sb("gst", [3, WHEADS])

        s_sh, s_shr = sem("shift_columns_ready"), sem("shift_rows_out")
        s_xi = sem("mixed_ready")
        s_sg = sem("decay_rate_gate_ready")
        s_rkv = sem("rkv_ready")
        s_kk, s_kksq, s_kkn, s_kkr = sem("kk_ready"), sem("kk_squares_ready"), sem("kk_norm_ready"), sem("kk_root_ready")
        s_rk = sem("rk_products_ready")
        s_dc, s_ex, s_exu = sem("decay_sums_ready"), sem("decay_exp_ready"), sem("decay_exp_used")
        s_wkv = sem("wkv_operands_ready")
        s_raw0, s_raw = sem("raw_zero"), [sem("raw_loaded0"), sem("raw_loaded1")]
        s_sq = sem("squares_ready")
        s_gn, s_gnr, s_yn = sem("gn_var_ready"), sem("gn_root_ready"), sem("y_normed")
        s_atm, s_sam, s_kept = sem("seq_masked_ready"), sem("sa_and_v_masked"), sem("states_decayed")
        s_v2 = sem("v_rows_again")
        s_stout = [sem("state_out0"), sem("state_out1")]
        s_wy = sem("mixer_rows_ready")

        s_par, s_x, s_keys = sem("par_loaded"), sem("x_loaded"), sem("keys_loaded")
        s_const = sem("consts_ready")
        s_out = sem("outputs_written")
        w_load = [sem(f"weights_loaded{i}") for i in range(WRING)]
        bank_ready = sem("bank_ready")
        bank_free = [sem(f"bank_free{i}") for i in range(BANKS)]
        s_silu = sem("silu_ready")
        s_xready = sem("x_ready")
        s_ms, s_rms = sem("mean_square_ready"), sem("rms_ready")
        s_h = sem("h_ready")
        s_gates = sem("conv_gates_ready")
        s_cv = sem("conv_ready")
        s_cout = sem("conv_state_ready")
        s_crow = sem("conv_rows_ready")
        s_kt = sem("keys_turned")
        s_q = sem("queries_ready")
        s_qp = sem("sample_queries_ready")
        s_qz = sem("padding_zero")
        s_hp = sem("prompt_h_ready")
        s_hn = sem("normed_ready")
        s_scur = sem("unit_scores_ready")
        s_sel, s_selgo = sem("selection_steps"), sem("selection_goes_on")
        s_actgo = sem("unit_copies_started")
        s_gexp = sem("gate_exp_ready")
        s_hs4 = sem("sample_h_repeated")
        s_htok = sem("h_rows_ready")
        s_vidx = sem("v_indices_ready")
        u_land = [sem(f"u_landed{i}") for i in range(RING)]
        v_land = [sem(f"v_landed{i}") for i in range(RING)]
        s_z = sem("z_done")
        s_gelu = sem("gelu_ready")
        s_coef = sem("coef_ready")
        s_diag = sem("diag_ready")
        v_free = sem("v_slots_free")
        acc_free = sem("acc_free")
        s_go = sem("gather_steps")
        s_acc = sem("expert_rows_ready")
        s_yt = sem("y_rows_ready")
        dve_step, act_step, pool_step = sem("dve_step"), sem("act_step"), sem("pool_step")

        tiles = []

        def weight_tiles(w, k, cols, group0, per):
            for j in range(cols // 512):
                tiles.append(([(None, w[:, j * 512:(j + 1) * 512].rearrange("(c p) m -> p c m", p=P))],
                              group0 + per * (j + 1) - 1))

        def ada_rows(j):
            return max(2 * j - 1, 0)

        def ada_cols(j, n):
            return 2 * j + 2 if j < n - 1 else 2 * n - 1

        WT = {}
        WT["ada"] = len(tiles)
        weight_tiles(a["w_ada"][0], D, 6 * D, 0, 0)
        weight_tiles(a["w_ada"][1][:, 0:4 * 512], D, 4 * 512, 0, 0)
        for t in range(16):
            tiles[t] = (tiles[t][0], GROUP["ada"] + ada_rows(t))
        WT["cin"] = len(tiles)
        weight_tiles(a["conv_w_in"][0], D, 3 * D, GROUP["cin"], 4)
        WT["cout"] = len(tiles)
        weight_tiles(a["conv_w_out"][0], D, D, GROUP["cout"], 4)
        WT["q0"] = len(tiles)
        weight_tiles(a["peer_wq"][0], D, 2 * D, GROUP["q0"], 4)
        for name in ("wr", "wk", "wv"):
            WT[name] = len(tiles)
            weight_tiles(a["rwkv_" + name][0], D, D, GROUP[name[1] + "p"], 4)
        WT["l1"] = len(tiles)
        tiles.append(([(lambda _: L1[:, :, 0:LW_], a["rwkv_w1"][0].rearrange("(c p) m -> p c m", p=P)),
                       (lambda _: L1[:, :, LW_:LW_ + LA_], a["rwkv_a1"][0].rearrange("(c p) m -> p c m", p=P)),
                       (lambda _: L1[:, :, LW_ + LA_:], a["rwkv_g1"][0].rearrange("(c p) m -> p c m", p=P))],
                      GROUP["lm"] + 2))
        WT["l2"] = len(tiles)
        tiles.append(([(lambda _: L2[0:LW_, 0, :], a["rwkv_w2"][0]), (lambda _: L2[0:LA_, 1, :], a["rwkv_a2"][0]),
                       (lambda _: L2[:, 2, :], a["rwkv_g2"][0])], GROUP["l2"] + 23))
        assert WT["wr"] % WRING == 0 and WT["l1"] % WRING == 2 and WT["l2"] % WRING == 3
        WT["adb"] = len(tiles)
        weight_tiles(a["w_ada"][1][:, 4 * 512:], D, 8 * 512, 0, 0)
        for j in range(8):
            tiles[WT["adb"] + j] = (tiles[WT["adb"] + j][0], GROUP["adb"] + ada_rows(j))
        WT["wo"] = len(tiles)
        weight_tiles(a["rwkv_wo"][0], D, D, GROUP["wo"], 4)
        WT["q1"] = len(tiles)
        weight_tiles(a["peer_wq"][1], D, 2 * D, GROUP["q1"], 4)
        load_val, _seen = [], [0] * WRING
        for t, (parts, _) in enumerate(tiles):
            _seen[t % WRING] += 16 * len(parts)
            load_val.append(_seen[t % WRING])

        def slot(h):
            return h % 2 * DC + h // 2

        block = ctx.enter_context(nc.Block())

        def col(name, i=0):
            return PAR[:, ROWS[name] + i:ROWS[name] + i + 1]

        def cols(name, n):
            return PAR[:, ROWS[name]:ROWS[name] + n]

        def shift_of(which):
            return ADA[:, which // 2, 24 * (which % 2):24 * (which % 2) + 8, :]

        def scale_of(which):
            return ADA[:, which // 2, 24 * (which % 2) + 8:24 * (which % 2) + 16, :]

        def gate_of(which):
            return ADA[:, which // 2, 24 * (which % 2) + 16:24 * (which % 2) + 24, :]

        def at(v, i):
            return v[:, bass.ds(i, 1), :].rearrange("p a n -> p (a n)")

        def per_step(v):
            v = v[:, :, 1:NCOND].unsqueeze(3)
            return v.broadcast_to([P, v.shape[1], NSEQ, NSTEP])

        def sample(v):
            return v[:, :, NP_TOK:TOK].rearrange("p c (b t) -> p c b t", b=NSEQ)

        @block.sync
        def _(sp):
            def rows_in(name, src, n):
                at = ROWS[name]
                sp.dma_start(PR[at % P:at % P + n, at // P, :], src).then_inc(s_par, 16)

            rows_in("g_mix", a["g_mix"].rearrange("l (c p) -> (l c) p", p=P), 16)
            rows_in("g_ffn", a["g_ffn"].rearrange("l (c p) -> (l c) p", p=P), 16)
            rows_in("g_final", a["g_final"].rearrange("(c p) -> c p", p=P), 8)
            rows_in("conv_k", a["conv_k"].rearrange("l w (c p) -> (l w c) p", p=P), 24)
            rows_in("rwkv_mix", a["rwkv_mix"].rearrange("l w (c p) -> (l w c) p", p=P), 48)
            for name in ("rwkv_w0", "rwkv_a0", "rwkv_k_k", "rwkv_k_a", "rwkv_lnw", "rwkv_lnb"):
                rows_in(name, a[name].rearrange("l (c p) -> (l c) p", p=P), 8)
            rows_in("rwkv_r_k", a["rwkv_r_k"].rearrange("l (c h) n -> (l c) (h n)", h=2), 8)
            rows_in("b_ada0", a["b_ada"][0].rearrange("(c p) -> c p", p=P), 48)
            rows_in("b_ada1", a["b_ada"][1].rearrange("(c p) -> c p", p=P), 48)
            def raw(c):
                for hp in range(2):
                    sp.dma_start(RAW[HS * hp:HS * (hp + 1), c % 2, :, HS * hp:HS * (hp + 1)],
                                 a["state_wkv"][0, :, 2 * c + hp].rearrange("b i j -> i b j")).then_inc(s_raw[c % 2], 16)

            for t, (parts, _) in enumerate(tiles):
                if t >= WRING:
                    sp.wait_ge(bank_ready, tiles[t - WRING][1] + 1)
                if t == WT["wo"]:
                    sp.wait_ge(s_raw0, 1)
                    for c in range(2):
                        raw(c)
                    sp.wait_ge(bank_ready, GROUP["sq2"])
                    sp.wait_ge(bank_free[(GROUP["sq2"] - 1) % BANKS], (GROUP["sq2"] - 1) // BANKS + 1)
                if t == WT["wk"]:
                    sp.wait_ge(s_sel, UNITS * NSEL)
                if t == WT["q1"]:
                    for c in range(2, DC):
                        sp.wait_ge(bank_ready, GROUP["sq2"] + SQ2.index(("turn1", c - 2)) + 1)
                        raw(c)
                    sp.wait_ge(bank_ready, GROUP["gn2"])
                    sp.wait_ge(bank_free[(GROUP["gn2"] - 1) % BANKS], (GROUP["gn2"] - 1) // BANKS + 1)
                for dst, src in parts:
                    sp.dma_start(W[:, t % WRING] if dst is None else dst(t % WRING), src).then_inc(w_load[t % WRING], 16)
            sp.wait_ge(s_out, 16 * 3)

        @block.tensor
        def _(pe):
            state = {"n": 0}

            def group(stage, j):
                n = state["n"]
                assert n == GROUP[stage] + j, (stage, j, n)
                state["n"] += 1
                if n >= BANKS:
                    pe.wait_ge(bank_free[n % BANKS], n // BANKS)
                return ps[:, n % BANKS, :]

            def done(ins):
                ins.then_inc(bank_ready, 1)

            def load_wait(t):
                pe.wait_ge(w_load[t % WRING], load_val[t])

            pe.wait_ge(s_const, 1)
            pe.wait_ge(s_par, 16 * 14)
            o = group("par", 0)
            for i, n in enumerate(PAR_ROWS):
                m = pe.transpose(o[:, i * P:i * P + n], PR[0:n, i, :], ident[0:n, 0:n])
            done(m)
            pe.wait_ge(s_x, 16 * 7)
            o = group("crow", 0)
            for c in range(DC):
                m = pe.transpose(o[:, c * CR_N:(c + 1) * CR_N], CRAW[0:CR_N, c * P:(c + 1) * P], ident[0:CR_N, 0:CR_N])
            done(m)
            for c in range(DC):
                o = group("x", c)
                for i in range(2):
                    pe.transpose(o[:, i * P:(i + 1) * P], XR[:, i, c * P:(c + 1) * P], ident[:])
                m = pe.transpose(o[:, NP_TOK:TOK], XR[0:NS_TOK, 2, c * P:(c + 1) * P], ident[0:NS_TOK, 0:NS_TOK])
                done(m)
            def ada(stage, wt, n):
                def turn(j):
                    o = group(stage, ada_cols(j, n))
                    nr = GROUP[stage] + ada_rows(j)
                    pe.wait_ge(bank_free[nr % BANKS], nr // BANKS + 1)
                    for m4 in range(4):
                        m = pe.transpose(o[:, m4 * NCOND:(m4 + 1) * NCOND], ADR[j % 2][0:NCOND, m4 * P:(m4 + 1) * P],
                                         ident[0:NCOND, 0:NCOND])
                    done(m)

                for j in range(n):
                    t = WT[wt] + j
                    load_wait(t)
                    o = group(stage, ada_rows(j))
                    for k in range(DC):
                        m = pe.matmul(o[0:NCOND, :], CT[:, k, 0:NCOND], W[:, t % WRING, k, :], start=(k == 0), stop=(k == DC - 1))
                    done(m)
                    if j > 0:
                        turn(j - 1)
                turn(n - 1)

            pe.wait_ge(s_silu, 2)
            ada("ada", "ada", 16)

            def norm(i):
                o = group(f"nrm{i}", 0)
                for c in range(DC):
                    pe.wait_ge(s_sq, DC * i + c + 1)
                    m = pe.matmul(o[:, 0:TOK], ones[:], SQ[:, c, :], start=(c == 0), stop=(c == DC - 1))
                done(m)

            def project(stage, wt, n_out, rhs):
                for m0 in range(n_out):
                    t = WT[wt] + m0 // 4
                    if m0 % 4 == 0:
                        load_wait(t)
                    o = group(stage, m0)
                    for k in range(DC):
                        m = pe.matmul(o[:, 0:TOK], W[:, t % WRING, k, (m0 % 4) * P:(m0 % 4 + 1) * P], rhs[:, k, :],
                                      start=(k == 0), stop=(k == DC - 1))
                    done(m)

            def normed(i):
                pe.wait_ge(s_hp, DC * (i + 1))
                pe.wait_ge(s_h, i + 1)

            norm(0)
            normed(0)
            project("cin", "cin", 24, H)
            pe.wait_ge(s_cv, 1)
            project("cout", "cout", DC, CV)
            pe.wait_ge(s_cout, 1)
            for i in range(2):
                o = group("cst", i)
                for c in range(4):
                    m = pe.transpose(o[0:18, c * P:(c + 1) * P], COUT[:, 4 * i + c, :], ident[:])
                done(m)

            def experts(layer):
                norm(2 * layer + 1)
                pe.wait_ge(s_keys, 16 * 2 * (layer + 1))
                for i in range(4):
                    o = group(f"kt{layer}", i)
                    for j in range(4):
                        m = pe.transpose(o[:, j * P:(j + 1) * P], KR[:, i // 2, 4 * (i % 2) + j, :], ident[:])
                    done(m)
                normed(2 * layer + 1)
                project(f"q{layer}", f"q{layer}", 16, H)
                pe.wait_ge(s_kt, 4 * (layer + 1))
                pe.wait_ge(s_q, 16 * (layer + 1))
                n = 0
                for tile in range(2):
                    for half in range(2):
                        for h4 in range(2):
                            o = group(f"sc{layer}", n)
                            n += 1
                            for j in range(4):
                                h = 4 * h4 + j
                                m = pe.matmul(o[:, j * P:(j + 1) * P], Q[:, 2 * h + half, tile * P:(tile + 1) * P],
                                              KT[:, half, h, :], start=True, stop=True)
                            done(m)
                pe.wait_ge(s_qp, layer + 1)
                o = group(f"sc{layer}", n)
                for half in range(2):
                    for e in range(2):
                        for g in range(4):
                            h = 2 * g + e
                            m = pe.matmul(o[:, (2 * half + e) * P:(2 * half + e + 1) * P], QP[:, 2 * h + half, :],
                                          KT[:, half, h, :], start=(g == 0), stop=(g == 3))
                done(m)
                pe.wait_ge(s_hs4, layer + 1)
                for tile in range(3):
                    for i in range(2):
                        o = group(f"ht{layer}", 2 * tile + i)
                        for j in range(4):
                            c = 4 * i + j
                            src = H[:, c, tile * P:(tile + 1) * P] if tile < 2 else HS4[:, c, :]
                            m = pe.transpose(o[:, j * P:(j + 1) * P], src, ident[:])
                        done(m)

                if layer == 0:
                    pe.sem_inc(v_free, RING)
                    pe.sem_inc(acc_free, 2)
                u0 = layer * UNITS

                def unit(u, e):
                    pe.wait_ge(acc_free, u + 1)
                    for k in range(TOPK):
                        pe.wait_ge(v_land[k % RING], u * 32 + 16 * (k // RING + 1))
                        pe.wait_ge(s_diag, u * 16 + (k + 1))
                        for i in range(2):
                            m = pe.matmul(ps[:, 4 + 2 * e + i, :], DG[:, k % NDIAG, :],
                                          RVV[:, k % RING, i * 512:(i + 1) * 512], start=(k == 0), stop=(k == TOPK - 1))
                        m.then_inc(v_free, 1)

                with pe.Fori(0, UNITS // 2 - 1) as i:
                    for e in range(2):
                        unit(i * 2 + (u0 + e), e)
                for e in range(2):
                    unit(u0 + UNITS - 2 + e, e)
                pe.wait_ge(s_acc, layer + 1)
                for c in range(DC):
                    o = group(f"res{layer}", c)
                    for i in range(2):
                        pe.matmul(o[:, i * P:(i + 1) * P], OACC[:, i, c * P:(c + 1) * P], ident[:], start=True, stop=True)
                    m = pe.matmul(o[:, NP_TOK:TOK], OACC[:, 2, c * P:(c + 1) * P], sel[:], start=True, stop=True)
                    done(m)

            def evac(stage, j):
                n = GROUP[stage] + j
                pe.wait_ge(bank_free[n % BANKS], n // BANKS + 1)

            def rwkv():
                pe.wait_ge(s_const, 2)
                normed(2)
                pe.wait_ge(s_sh, 1)
                for i in range(2):
                    o = group("sst", i)
                    for c in range(4):
                        m = pe.transpose(o[0:NCOND, c * P:(c + 1) * P], COUT[:, 4 * i + c, 0:NCOND], ident[:])
                    done(m)
                for i, (stage, wt) in enumerate((("rp", "wr"), ("kp", "wk"), ("vp", "wv"))):
                    pe.wait_ge(s_xi, i + 1)
                    project(stage, wt, DC, (XI0, XI1)[i % 2])
                load_wait(WT["l1"])
                at0 = 0
                for i, n in enumerate((LW_, LA_, LG_)):
                    pe.wait_ge(s_xi, 4 + i)
                    o = group("lm", i)
                    for k in range(DC):
                        m = pe.matmul(o[0:n, 0:TOK], L1[:, k, at0:at0 + n], (XI1, XI0)[i % 2][:, k, :],
                                      start=(k == 0), stop=(k == DC - 1))
                    done(m)
                    at0 += n
                load_wait(WT["l2"])
                for i, n in enumerate((LW_, LA_, LG_)):
                    evac("lm", i)
                    for c in range(DC):
                        o = group("l2", DC * i + c)
                        done(pe.matmul(o[:, 0:TOK], L2[0:n, i, c * P:(c + 1) * P], LM[0:n, i, :], start=True, stop=True))
                pe.wait_ge(s_kksq, 1)
                for c in range(DC):
                    o = group("kn", c)
                    done(pe.matmul(o[:, 0:TOK], BLK, XI1[:, c, :], start=True, stop=True))
                pe.wait_ge(s_rk, 1)
                for c in range(DC):
                    o = group("bn", c)
                    done(pe.matmul(o[:, 0:TOK], BLK, XI1[:, c, :], start=True, stop=True))
                ada("adb", "adb", 8)
                pe.wait_ge(s_wkv, 1)
                for tile in range(3):
                    n = P if tile < 2 else NS_TOK
                    t0 = tile * P
                    for i in range(3):
                        for q in range(2):
                            o = group(f"tm{tile}", 2 * i + q)
                            for j in range(4):
                                c = 4 * q + j
                                src = (VF, BF, KF)[i][:, c, t0:t0 + n] if tile < 2 or i == 0 else BBS[:, i - 1, c, :]
                                m = pe.transpose(o[0:n, j * P:(j + 1) * P], src, ident[:])
                            done(m)
                    nm = f"nm{tile}"
                    steps = NM_STEPS if tile < 2 else NM_STEPS_S

                    def head(f, h):
                        return f[HS * (h % 2):HS * (h % 2) + HS, h // 2, t0:t0 + n]

                    for bp in range(2):
                        for step in range(steps):
                            for b in range(2):
                                def need(*which):
                                    for w in which:
                                        evac(nm, (bp * steps + w) * 2 + b)

                                o = group(nm, (bp * steps + step) * 2 + b)
                                T = NT[0:n, b, :, :, 0:n]
                                heads = [2 * (4 * bp + j) + b for j in range(4)]
                                G = (GG[0:n, 3] if tile < 2 else GS[3][0:n])[:, slot(heads[0]):slot(heads[0]) + 4, :]
                                A8, U8, A2, U2, TT = (T[:, i] for i in range(5))
                                if step < 5:
                                    ops = [(BF, AF), (AF, BF), (KF, AF), (BF, RF), (KF, RF)][step]
                                    for j, h in enumerate(heads):
                                        m = pe.matmul(o[0:n, j * n:(j + 1) * n], head(ops[0], h), head(ops[1], h),
                                                      start=True, stop=True)
                                    done(m)
                                    continue
                                if tile == 2:
                                    if step == 5:
                                        need(0, 1)
                                    else:
                                        need(5)
                                    l, r = {5: (U8, A8), 6: (A2, G)}[step]
                                else:
                                    need(*{5: (0, 1), 7: (6,), 8: (5,), 11: (10, 7), 12: (9, 8), 13: (11,), 14: (12, 13),
                                           16: (14,), 17: (15, 16), 19: (17,), 20: (18, 19)}.get(step, ()))
                                    l, r = {5: (A8, U8), 6: (U8, A8), 7: (A2, G), 8: (U2, TT), 9: (A2, U2), 10: (U2, A2),
                                            11: (A8, G), 12: (U8, TT), 13: (T[:, 5], G), 14: (TT, A2), 15: (A2, TT),
                                            16: (T[:, 6], G), 17: (TT, A2), 18: (A2, TT), 19: (T[:, 7], G),
                                            20: (TT, A2)}[step]
                                for j in range(4):
                                    m = pe.matmul(o[0:n, j * n:(j + 1) * n], l[:, j, :], r[:, j, :], start=True, stop=True)
                                done(m)
                    for bp in range(2):
                        for b in range(2):
                            evac(nm, (bp * steps + steps - 1) * 2 + b)
                            for w in (2, 3, 4):
                                evac(nm, (bp * steps + w) * 2 + b)
                    for j in range(6):
                        evac(f"tm{tile}", j)
                    if tile < 2:
                        sq = f"sq{tile}"
                        for ch in range(2):
                            rows = slice(HS * ch, HS * ch + HS)
                            if ch == 0 and tile == 0:
                                pe.wait_ge(s_wkv, 2)
                            elif ch == 0:
                                evac("sq0", 14)
                                evac("sq0", 15)
                            else:
                                evac(sq, 6)
                                evac(sq, 7)
                            for q in range(2):
                                o = group(sq, 8 * ch + q)
                                for j in range(4):
                                    c = 4 * q + j
                                    pe.matmul(o[:, j * P:(j + 1) * P], AF[:, c, t0:t0 + P], SB[:, c, :], start=True, stop=False,
                                              skip_group_check=True)
                                    for hp in range(2):
                                        h = 2 * c + hp
                                        m = pe.matmul(o[:, h % 8 * HS:h % 8 * HS + HS], GG[:, 0, slot(h), :], VT[:, h * HS:(h + 1) * HS],
                                                      start=False, stop=True, skip_group_check=True)
                                done(m)
                            for q in range(2):
                                evac(sq, 8 * ch + q)
                                o = group(sq, 8 * ch + 2 + q)
                                for j in range(8):
                                    h = 8 * q + j
                                    m = pe.matmul(o[:, j * HS:(j + 1) * HS], GG[:, 3, slot(h), :], RH[:, h // 2, HS * (h % 2):HS * (h % 2) + HS],
                                                  start=True, stop=True)
                                done(m)
                            for q in range(2):
                                evac(sq, 8 * ch + 2 + q)
                                o = group(sq, 8 * ch + 4 + q)
                                for j in range(4):
                                    c = 4 * q + j
                                    pe.matmul(o[:, j * P:(j + 1) * P], RF[:, c, t0:t0 + P], SB[:, c, :], start=True, stop=False,
                                              skip_group_check=True)
                                    for hp in range(2):
                                        h = 2 * c + hp
                                        oh = o[:, h % 8 * HS:h % 8 * HS + HS]
                                        pe.matmul(oh, GG[:, 1, slot(h), :], SA[:, c, HS * hp:HS * hp + HS], start=False, stop=False,
                                                  skip_group_check=True)
                                        m = pe.matmul(oh, GG[:, 2, slot(h), :], VT[:, h * HS:(h + 1) * HS], start=False, stop=True,
                                                      skip_group_check=True)
                                done(m)
                            for q in range(2):
                                o = group(sq, 8 * ch + 6 + q)
                                for j in range(4):
                                    c = 4 * q + j
                                    oc = o[:, j * P:(j + 1) * P]
                                    pe.matmul(oc, ident[:], SB[:, c, :], start=True, stop=False)
                                    pe.matmul(oc, BT[rows, c * P:(c + 1) * P], SA[rows, c, :], start=False, stop=False)
                                    m = pe.matmul(oc, KTK[rows, c * P:(c + 1) * P], VT[rows, c * P:(c + 1) * P], start=False, stop=True)
                                done(m)
                        if tile == 1:
                            evac(sq, 14)
                            evac(sq, 15)
                            for q in range(2):
                                o = group("pso", q)
                                for j in range(4):
                                    m = pe.transpose(o[:, j * P:(j + 1) * P], SB[:, 4 * q + j, :], ident[:])
                                done(m)
                    else:
                        def sample_step(kind, c):
                            o = group("sq2", SQ2.index((kind, c)))
                            def pair(o, lhsT, rhs, start):
                                for hp in range(2):
                                    m = pe.matmul(o[:, HS * hp:HS * hp + HS], lhsT(slot(2 * c + hp)), rhs[:, HS * hp:HS * hp + HS],
                                                  start=start, stop=True, skip_group_check=True)
                                return m

                            if kind in ("turn0", "turn1"):
                                half = int(kind[-1])
                                if half == 0:
                                    pe.wait_ge(s_raw[c % 2], 32 * (c // 2 + 1))
                                for j in range(4):
                                    m = pe.transpose(o[:, j * P:(j + 1) * P], RAW[:, c % 2, 4 * half + j, :], ident[:])
                            elif kind == "right":
                                pe.wait_ge(s_atm, c + 1)
                                evac("sq2", SQ2.index(("turn0", c)))
                                evac("sq2", SQ2.index(("turn1", c)))
                                o = o[0:2 * n, 0:P]
                                for q in range(NSEQ):
                                    pe.matmul(o, ART[:, c % 2, q].rearrange("p r t -> p (r t)"), SS[:, c % 2, q, :],
                                              start=(q == 0), stop=False, skip_group_check=True)
                                m = pair(o, lambda h: GKV[0:n, h].rearrange("p r t -> p (r t)"), VT[0:n, c * P:(c + 1) * P], False)
                            elif kind == "sa":
                                evac("sq2", SQ2.index(("right", c)))
                                m = pair(o[0:n], lambda h: GS[3][0:n, h, :], RHS[0:n], True)
                            elif kind == "y":
                                evac("sq2", SQ2.index(("sa", c)))
                                m = pair(o[0:n], lambda h: GS[1][0:n, h, :], SAV[0:n, c * P:(c + 1) * P], True)
                            elif kind in ("new0", "new1"):
                                half = int(kind[-1])
                                pe.wait_ge(s_sam, c + 1)
                                m = pe.matmul(o, BT[0:2 * n, c * P:(c + 1) * P],
                                              SAVM[0:2 * n, 4 * half:4 * half + 4, :].rearrange("p s n -> p (s n)"), start=True, stop=True)
                            else:
                                half = int(kind[-1])
                                evac("sq2", SQ2.index((f"new{half}", c)))
                                for j in range(4):
                                    m = pe.transpose(o[:, j * P:(j + 1) * P], NEW[:, c % 2, 4 * half + j, :], ident[:])
                            done(m)

                        for kind, c in SQ2:
                            sample_step(kind, c)
                    pe.wait_ge(s_yn, tile + 1)
                    for q in range(2):
                        o = group(f"gn{tile}", q)
                        for j in range(4):
                            m = pe.transpose(o[:, j * n:(j + 1) * n], YR[0:n, (4 * q + j) * P:(4 * q + j + 1) * P], ident[0:n, 0:n])
                        done(m)
                pe.wait_ge(s_wy, 1)
                project("wo", "wo", DC, H)

            experts(0)
            norm(2)
            rwkv()
            experts(1)
            norm(4)
            pe.wait_ge(s_h, 5)
            for tile in range(3):
                n = P if tile < 2 else NS_TOK
                for i in range(2):
                    o = group("fin", 2 * tile + i)
                    for j in range(4):
                        m = pe.transpose(o[0:n, j * P:(j + 1) * P], H[:, 4 * i + j, tile * P:tile * P + n], ident[:])
                    done(m)

        @block.scalar
        def _(act):
            A = Steps(act, act_step)
            act.dma_start(CRAW[CR_COND:CR_COND + 1, :], a["c_prompt"]).then_inc(s_x, 16)
            act.dma_start(CRAW[CR_COND + 1:CR_COND + NCOND, :], a["c_sample"]).then_inc(s_x, 16)
            act.dma_start(CRAW[CR_CONV:CR_CONV + 16, :], a["state_conv"].rearrange("l b w d -> (l b w) d")).then_inc(s_x, 16)
            act.dma_start(CRAW[CR_SHIFT:CR_SHIFT + 8, :], a["state_shift"].rearrange("l b d -> (l b) d")).then_inc(s_x, 16)
            for i in range(2):
                act.dma_start(XR[:, i, :], a["x_prompt"][0, i * P:(i + 1) * P, :]).then_inc(s_x, 16)
            act.dma_start(XR[0:NS_TOK, 2, :], a["x_sample"].rearrange("b t d -> (b t) d")).then_inc(s_x, 16)

            def take(stage, j):
                n = GROUP[stage] + j
                act.wait_ge(bank_ready, n + 1)
                return ps[:, n % BANKS, :], bank_free[n % BANKS]

            o, free = take("crow", 0)
            ov = o[:, 0:DC * CR_N].rearrange("p (c n) -> p c n", c=DC)
            act.activation(CT[:, :, 0:NCOND], ov[:, :, 0:NCOND], ACT.Silu).then_inc(s_silu, 1)
            act.activation(CT[:, :, NCOND:CR_N], ov[:, :, NCOND:CR_N], ACT.Copy).then_inc(s_silu, 1)
            act.wait_ge(s_silu, 2)
            act.sem_inc(free, 1)

            def copy(stage, j, dst, src=lambda o: o, func=ACT.Copy, **kw):
                o, free = take(stage, j)
                act.activation(dst, src(o), func, **kw).then_inc(free, 1)

            def taken(stage, j):
                n = GROUP[stage] + j
                act.wait_ge(bank_free[n % BANKS], n // BANKS + 1)

            def ada(stage, n, layer_and_chunk):
                def columns(j):
                    o, free = take(stage, ada_cols(j, n))
                    for m4 in range(4):
                        layer, m0 = layer_and_chunk(j)
                        m = act.activation(ADA[:, layer, m0 + m4, :], o[:, m4 * NCOND:(m4 + 1) * NCOND], ACT.Identity,
                                           bias=col(f"b_ada{layer}", m0 + m4))
                    m.then_inc(free, 1)

                for j in range(n):
                    copy(stage, ada_rows(j), ADR[j % 2][0:NCOND, :], lambda o: o[0:NCOND, :])
                    if j > 0:
                        columns(j - 1)
                columns(n - 1)

            act.wait_ge(bank_free[0], 1)
            ada("ada", 16, lambda j: (j // 12, 4 * (j % 12)))

            def squares(i):
                for c in range(DC):
                    act.wait_ge(s_xready, DC * i + c + 1)
                    act.activation(SQ[:, c, :], X[:, c, :], ACT.Square).then_inc(s_sq, 1)
                act.wait_ge(s_ms, i + 1)
                act.activation(rms[:], rms[:], ACT.Sqrt).then_inc(s_rms, 1)
                if i < 4:
                    for c in range(DC):
                        act.wait_ge(s_hn, DC * i + c + 1)
                        act.activation(H[:, c, 0:NP_TOK], HN[:, c, 0:NP_TOK], ACT.Identity, scale=GA[:, i, c, 0:1],
                                       bias=shift_of(i)[:, c, 0:1]).then_inc(s_hp, 1)

            squares(0)
            act.wait_ge(s_h, 1)
            for m in range(16):
                o, free = take("cin", m)
                dst = (BG if m < 8 else CG)[:, m % 8, :]
                act.activation(dst, o[:, 0:TOK], ACT.Copy).then_inc(free, 1)
                if m == 15:
                    act.wait_ge(free, (GROUP["cin"] + m) // BANKS + 1)
                    act.sem_inc(s_gates, 1)
            for i in range(2):
                o, free = take("cst", i)
                if i == 0:
                    act.wait_ge(s_cv, 1)
                act.activation(CROW[0:18, i * 512:(i + 1) * 512], o[0:18, :], ACT.Copy).then_inc(free, 1)
                act.wait_ge(free, (GROUP["cst"] + i) // BANKS + 1)
            act.dma_start(out[2].rearrange("l b w d -> (l b w) d"), CROW[0:2, :]).then_inc(s_crow, 16)
            act.dma_start(out[5].rearrange("l b w d -> (l b w) d"), CROW[2:18, :]).then_inc(s_crow, 16)

            def experts(layer):
                squares(2 * layer + 1)
                act.wait_ge(bank_ready, GROUP[f"nrm{2 * layer + 1}"] + 1)
                for half, k in enumerate(("peer_k1", "peer_k2")):
                    act.dma_start(KR[:, half, :, :], a[k][layer].rearrange("h k d -> k h d")).then_inc(s_keys, 16)
                act.wait_ge(s_h, 2 * layer + 2)
                act.wait_ge(s_hp, DC * (2 * layer + 2))
                for i in range(4):
                    o, free = take(f"kt{layer}", i)
                    act.activation(KT[:, i // 2, 4 * (i % 2):4 * (i % 2) + 4, :],
                                   o.rearrange("p (h k) -> p h k", h=4), ACT.Copy).then_inc(s_kt, 1)
                    act.wait_ge(s_kt, 4 * layer + i + 1)
                    act.sem_inc(free, 1)
                for m in range(16):
                    o, free = take(f"q{layer}", m)
                    act.activation(Q[:, m, :], o[:, 0:TOK], ACT.Copy).then_inc(s_q, 1)
                    act.wait_ge(s_q, 16 * layer + m + 1)
                    act.sem_inc(free, 1)
                for n in range(8):
                    tile, half, h4 = n // 4, (n // 2) % 2, n % 2
                    copy(f"sc{layer}", n, SCALL[:, 8 * tile + 4 * h4:8 * tile + 4 * h4 + 4, half * NKEYS:(half + 1) * NKEYS],
                         lambda o: o.rearrange("p (h k) -> p h k", h=4))
                    if n == 3:
                        for j in range(4):
                            taken(f"sc{layer}", j)
                        for e in range(2):
                            act.activation(SCUR[:, e].rearrange("p a k -> p (a k)"), SCALL[:, e, :], ACT.Copy).then_inc(s_scur, 1)
                copy(f"sc{layer}", 8, SCALL[:, 16:18, :].rearrange("p e (a k) -> p a e k", a=2),
                     lambda o: o.rearrange("p (a e k) -> p a e k", a=2, e=2))
                for tile in range(3):
                    for i in range(2):
                        copy(f"ht{layer}", 2 * tile + i, HTOK[:, tile, i * 512:(i + 1) * 512])
                for j in range(9):
                    taken(f"sc{layer}", j)

                u0 = layer * UNITS

                def gate_exp(u, e):
                    act.wait_ge(s_sel, u * NSEL + SEL_IDX)
                    act.activation(GATE[:, e, :], GATE[:, e, :], ACT.Exp).then_inc(s_gexp, 1)

                for e in range(2):
                    gate_exp(u0 + e, e)

                def unit(u, lu, e, last):
                    if not last:
                        act.wait_ge(s_sel, u * NSEL + NSEL)
                        act.sem_inc(s_actgo, 1)
                        act.activation(SCUR[:, e].rearrange("p a k -> p (a k)"), at(SCALL, lu + 2), ACT.Copy).then_inc(s_scur, 1)
                    act.wait_ge(s_z, u * 16 + 16)
                    act.activation(GL[:, e, :], ZB[:, e, :], ACT.Gelu).then_inc(s_gelu, 1)
                    act.wait_ge(s_coef, u + 1)
                    for k in range(TOPK):
                        if k == 14 and not last:
                            gate_exp(u + 2, e)
                        act.wait_ge(v_free, u * 16 + (k + RING - NDIAG + 1))
                        act.activation(DG[:, k % NDIAG, :], ident[:], ACT.Copy, scale=CF[:, e, k:k + 1]).then_inc(s_diag, 1)

                with act.Fori(0, UNITS // 2 - 1) as i:
                    for e in range(2):
                        unit(i * 2 + (u0 + e), i * 2 + e, e, False)
                for e in range(2):
                    unit(u0 + UNITS - 2 + e, UNITS - 2 + e, e, True)

            def rwkv():
                for i in range(2):
                    copy("sst", i, CROW2[0:NCOND, i * 512:(i + 1) * 512], lambda o: o[0:NCOND, :])
                    taken("sst", i)
                act.dma_start(out[3][0], CROW2[0:1, :]).then_inc(s_shr, 16)
                act.dma_start(out[6][0], CROW2[1:NCOND, :]).then_inc(s_shr, 16)
                for stage, dst in (("rp", RF), ("kp", KF), ("vp", VF)):
                    for c in range(DC):
                        copy(stage, c, dst[:, c, :], lambda o: o[:, 0:TOK])
                copy("lm", 0, LM[0:LW_, 0, :], lambda o: o[0:LW_, 0:TOK], ACT.Tanh)
                copy("lm", 1, LM[0:LA_, 1, :], lambda o: o[0:LA_, 0:TOK])
                copy("lm", 2, LM[0:LG_, 2, :], lambda o: o[0:LG_, 0:TOK], ACT.Sigmoid)
                for c in range(DC):
                    copy("l2", c, LW[:, c, :], lambda o: o[:, 0:TOK], ACT.Sigmoid, bias=col("rwkv_w0", c))
                for c in range(DC):
                    copy("l2", DC + c, BF[:, c, :], lambda o: o[:, 0:TOK], ACT.Sigmoid, bias=col("rwkv_a0", c))
                for c in range(DC):
                    copy("l2", 2 * DC + c, GF[:, c, :], lambda o: o[:, 0:TOK])
                for j in range(3):
                    taken("l2", 20 + j)
                taken("l2", 23)
                act.sem_inc(s_sg, 1)
                act.wait_ge(s_kk, 1)
                act.activation(XI1, AF, ACT.Square).then_inc(s_kksq, 1)
                act.wait_ge(s_kkn, 1)
                act.activation(XI0, XI0, ACT.Sqrt).then_inc(s_kkr, 1)
                ada("adb", 8, lambda j: (1, 16 + 4 * j))
                act.wait_ge(s_dc, 1)
                act.activation(XI1, XI0, ACT.Exp).then_inc(s_ex, 1)
                act.activation(FE[:], FE[:], ACT.Exp).then_inc(s_ex, 1)
                act.activation(EC[:], EC[:], ACT.Exp).then_inc(s_ex, 1)
                act.wait_ge(s_exu, 1)
                act.activation(XI1, XI0, ACT.Exp, scale=-1.0).then_inc(s_ex, 1)
                act.wait_ge(s_exu, 2)
                act.activation(LW, LW, ACT.Exp).then_inc(s_ex, 1)
                for tile in range(3):
                    n = P if tile < 2 else NS_TOK
                    for i in range(3):
                        for q in range(2):
                            dst = (VT, BT, KTK)[i][0:n] if tile < 2 or i < 2 else BT[n:2 * n]
                            copy(f"tm{tile}", 2 * i + q, dst[:, q * 512:(q + 1) * 512], lambda o: o[0:n, :])
                            if tile == 2 and i == 1 and q == 0:
                                for j in range(2):
                                    taken("tm2", j)
                                act.activation(SAV[n:2 * n, :], VT[0:n, :], ACT.Copy).then_inc(s_v2, 1)
                    steps = NM_STEPS if tile < 2 else NM_STEPS_S
                    to = {5: 3, 6: 2, 9: 1, 10: 0, 13: 2, 16: 2, 19: 2} if tile < 2 else {5: 2}
                    for bp in range(2):
                        for step in sorted(to):
                            for b in range(2):
                                copy(f"nm{tile}", (bp * steps + step) * 2 + b, NT[0:n, b, to[step], :, 0:n],
                                     lambda o: o[0:n, 0:4 * n].rearrange("p (h t) -> p h t", h=4))
                    if tile < 2:
                        for ch in range(2):
                            rows = slice(HS * ch, HS * ch + HS)
                            for q in range(2):
                                copy(f"sq{tile}", 8 * ch + q, RH[:, 4 * q:4 * q + 4, :], lambda o: o.rearrange("p (c i) -> p c i", c=4))
                            for q in range(2):
                                copy(f"sq{tile}", 8 * ch + 2 + q, SA[:, 4 * q:4 * q + 4, :], lambda o: o.rearrange("p (c i) -> p c i", c=4))
                            for q in range(2):
                                copy(f"sq{tile}", 8 * ch + 4 + q, YR[rows, q * 512:(q + 1) * 512], lambda o: o[rows, :])
                        if tile == 1:
                            for q in range(2):
                                copy("pso", q, PSO[:, 4 * q:4 * q + 4, :], lambda o: o.rearrange("p (c j) -> p c j", c=4))
                                taken("pso", q)
                            for hp in range(2):
                                act.dma_start(out[4][0, 0].rearrange("(c h) i j -> h i c j", h=2)[hp],
                                              PSO[HS * hp:HS * hp + HS, :, HS * hp:HS * hp + HS]).then_inc(s_shr, 16)
                    else:
                        act.wait_ge(s_shr, 64)
                        for kind, c in SQ2:
                            half = int(kind[-1]) if kind[-1].isdigit() else 0
                            four = lambda o: o.rearrange("p (s n) -> p s n", s=4)
                            if kind in ("turn0", "turn1"):
                                if half == 0 and c >= 2:
                                    act.wait_ge(s_kept, c - 1)
                                copy("sq2", SQ2.index((kind, c)), SS[:, c % 2, 4 * half:4 * half + 4, :], four)
                            elif kind in ("out0", "out1"):
                                if half == 0 and c >= 2:
                                    act.wait_ge(s_stout[c % 2], 32 * (c // 2))
                                copy("sq2", SQ2.index((kind, c)), OUTB[:, c % 2, 4 * half:4 * half + 4, :], four)
                                if half == 1:
                                    for k in ("out0", "out1"):
                                        taken("sq2", SQ2.index((k, c)))
                                    for hp in range(2):
                                        act.dma_start(out[7][0, :, 2 * c + hp].rearrange("b i j -> i b j"),
                                                      OUTB[HS * hp:HS * hp + HS, c % 2, :, HS * hp:HS * hp + HS]).then_inc(s_stout[c % 2], 16)
                    act.wait_ge(s_gn, tile + 1)
                    act.activation(gst[0:n, 1, :], gst[0:n, 1, :], ACT.Sqrt).then_inc(s_gnr, 1)
                for i in range(2):
                    act.wait_ge(s_stout[i], 16 * DC)

            experts(0)
            squares(2)
            rwkv()
            experts(1)
            squares(4)
            for tile in range(3):
                n = P if tile < 2 else NS_TOK
                for i in range(2):
                    o, free = take("fin", 2 * tile + i)
                    act.activation(YT[0:n, tile, i * 512:(i + 1) * 512], o[0:n, :], ACT.Copy).then_inc(s_yt, 1)
                    act.wait_ge(s_yt, 2 * tile + i + 1)
                    act.sem_inc(free, 1)
                dst = out[0][0, tile * P:(tile + 1) * P, :] if tile < 2 else out[1].rearrange("b t d -> (b t) d")
                act.dma_start(dst, YT[0:n, tile, :]).then_inc(s_out, 16)

        @block.vector
        def _(v):
            V = Steps(v, dve_step)

            def take(stage, j):
                n = GROUP[stage] + j
                v.wait_ge(bank_ready, n + 1)
                return ps[:, n % BANKS, :], bank_free[n % BANKS]

            def free_bank(free):
                V.sync()
                v.sem_inc(free, 1)

            v.wait_ge(s_const, 1)
            V.chain(v.tensor_tensor(sel[:], ident[:, 0:32], ident[:, 32:64], ALU.add))
            V.chain(v.tensor_tensor(sel[:], sel[:], ident[:, 64:96], ALU.add))
            V.chain(v.tensor_tensor(sel[:], sel[:], ident[:, 96:128], ALU.add))
            o, free = take("par", 0)
            for i, n in enumerate(PAR_ROWS):
                V.do(v.tensor_copy(PAR[:, i * P:i * P + n], o[:, i * P:i * P + n]))
            free_bank(free)
            for c in range(DC):
                o, free = take("x", c)
                V.do(v.tensor_copy(X[:, c, :], o[:, 0:TOK]))
                free_bank(free)
                v.sem_inc(s_xready, 1)

            def gains(stage, n, which):
                last = GROUP[stage] + ada_cols(n - 1, n)
                v.wait_ge(bank_free[last % BANKS], last // BANKS + 1)
                for w in which:
                    g = cols("g_mix", 16) if w % 2 == 0 else cols("g_ffn", 16)
                    g = g[:, 8 * (w // 2):8 * (w // 2) + 8].unsqueeze(2).broadcast_to([P, DC, NCOND])
                    V.do(v.scalar_tensor_tensor(GA[:, w], scale_of(w), 1.0, g, ALU.add, ALU.mult))
                V.sync()

            gains("ada", 16, (0, 1, 2))

            def norm(i):
                o, free = take(f"nrm{i}", 0)
                V.do(v.tensor_scalar(rms[:], o[:, 0:TOK], 1.0 / D, EPS, ALU.mult, ALU.add), s_ms)
                free_bank(free)
                v.wait_ge(s_rms, i + 1)
                V.chain(v.reciprocal(rstd[:], rms[:]))
                for c in range(DC):
                    V.do(v.tensor_tensor(HN[:, c, :], X[:, c, :], rstd[:], ALU.mult), s_hn if i < 4 else None)
                V.sync()
                if i < 4:
                    V.chain(v.tensor_tensor(sample(HN), sample(HN), per_step(GA[:, i]), ALU.mult))
                    V.chain(v.tensor_tensor(sample(H), sample(HN), per_step(shift_of(i)), ALU.add))
                else:
                    for c in range(DC):
                        V.do(v.tensor_scalar(H[:, c, :], HN[:, c, :], col("g_final", c), None, ALU.mult))
                    V.sync()
                v.sem_inc(s_h, 1)

            def residual(stage, which):
                g = gate_of(which)
                for c in range(DC):
                    o, free = take(stage, c)
                    V.do(v.scalar_tensor_tensor(X[:, c, 0:NP_TOK], o[:, 0:NP_TOK], g[:, c, 0:1], X[:, c, 0:NP_TOK],
                                                ALU.mult, ALU.add))
                    gs = g[:, c, 1:NCOND].unsqueeze(2).broadcast_to([P, NSEQ, NSTEP])
                    tv = tmpS[:, c % 2, :].rearrange("p (b t) -> p b t", b=NSEQ)
                    V.do(v.tensor_tensor(tv, o[:, NP_TOK:TOK].rearrange("p (b t) -> p b t", b=NSEQ), gs, ALU.mult))
                    free_bank(free)
                    V.do(v.tensor_tensor(X[:, c, NP_TOK:TOK], X[:, c, NP_TOK:TOK], tmpS[:, c % 2, :], ALU.add))
                    V.sync()
                    v.sem_inc(s_xready, 1)

            norm(0)
            sampleU = UH[:, :, NP_TOK + 2:].rearrange("p c (b t) -> p c b t", b=NSEQ)
            V.do(v.memset(UH[:, :, 0:2], 0.0))
            V.do(v.tensor_copy(sampleU[:, :, :, 0:2], CT[:, :, CR_CONV:CR_CONV + 16].rearrange("p c (b w) -> p c b w", b=NSEQ)))
            v.wait_ge(s_gates, 1)
            for c in range(DC):
                o, free = take("cin", 16 + c)
                V.do(v.tensor_tensor(UH[:, c, 2:NP_TOK + 2], o[:, 0:NP_TOK], CG[:, c, 0:NP_TOK], ALU.mult))
                V.do(v.tensor_tensor(sampleU[:, c, :, 2:6], o[:, NP_TOK:TOK].rearrange("p (b t) -> p b t", b=NSEQ),
                                     CG[:, c, NP_TOK:TOK].rearrange("p (b t) -> p b t", b=NSEQ), ALU.mult))
                free_bank(free)
            for j in range(3):
                for c in range(DC):
                    dst, src, k = CV[:, c, 0:NP_TOK], UH[:, c, j:j + NP_TOK], col("conv_k", 8 * j + c)
                    if j == 0:
                        V.do(v.tensor_scalar(dst, src, k, None, ALU.mult))
                    else:
                        V.do(v.scalar_tensor_tensor(dst, src, k, dst, ALU.mult, ALU.add))
                V.sync()
            cs = [CS[:, i].rearrange("p (c b t) -> p c b t", c=DC, b=NSEQ) for i in range(2)]
            for j in range(3):
                for c in range(DC):
                    k = col("conv_k", 8 * j + c)
                    if j == 0:
                        V.do(v.tensor_scalar(cs[0][:, c], sampleU[:, c, :, 0:4], k, None, ALU.mult))
                    else:
                        V.do(v.scalar_tensor_tensor(cs[0][:, c], sampleU[:, c, :, j:j + 4], k, cs[0][:, c], ALU.mult, ALU.add))
                V.sync()
            V.do(v.tensor_tensor(CV[:, :, 0:NP_TOK], CV[:, :, 0:NP_TOK], BG[:, :, 0:NP_TOK], ALU.mult))
            V.do(v.tensor_tensor(sample(CV), cs[0], sample(BG), ALU.mult))
            V.sync()
            v.sem_inc(s_cv, 1)
            V.do(v.tensor_copy(COUT[:, :, 0:2], UH[:, :, NP_TOK:NP_TOK + 2]))
            V.do(v.tensor_copy(COUT[:, :, 2:18].rearrange("p c (b w) -> p c b w", b=NSEQ), sampleU[:, :, :, 4:6]))
            V.sync()
            v.sem_inc(s_cout, 1)
            residual("cout", 0)

            def choose(u, e, layer):
                state = {"j": 0}

                def step(make, back=1):
                    j = state["j"]
                    state["j"] += 1
                    if not isinstance(u, int) or u * NSEL + j + 1 - back > 0:
                        v.wait_ge(s_sel, u * NSEL + (j + 1 - back))
                    v.sem_inc(s_selgo, 1)
                    make().then_inc(s_sel, 1)

                s0, s1 = SCUR[:, e, 0, :], SCUR[:, e, 1, :]
                r0, r1 = REST[:, 0, 0:NKEYS], REST[:, 1, 0:NKEYS]
                grid = [P, TOPK, TOPK]
                square = lambda x: x.rearrange("p (a b) -> p a b", a=TOPK)
                v.wait_ge(s_scur, u + 1)
                v.sem_inc(s_selgo, 1)
                step(lambda: v.max(VAL[:, 0, 0:8], s0))
                step(lambda: v.max(VAL[:, 1, 0:8], s1), 2)
                yield
                step(lambda: v.max_index(KEY[:, 0, 0:8], VAL[:, 0, 0:8], s0), 2)
                step(lambda: v.match_replace(r0, VAL[:, 0, 0:8], s0, NEG), 3)
                yield
                step(lambda: v.max_index(KEY[:, 1, 0:8], VAL[:, 1, 0:8], s1), 3)
                step(lambda: v.match_replace(r1, VAL[:, 1, 0:8], s1, NEG), 4)
                yield
                step(lambda: v.max(VAL[:, 0, 8:16], r0), 3)
                step(lambda: v.max(VAL[:, 1, 8:16], r1), 2)
                yield
                step(lambda: v.max_index(KEY[:, 0, 8:16], VAL[:, 0, 8:16], r0), 2)
                step(lambda: v.max_index(KEY[:, 1, 8:16], VAL[:, 1, 8:16], r1), 2)
                yield
                step(lambda: v.tensor_tensor(square(CAND), VAL[:, 0].unsqueeze(2).broadcast_to(grid),
                                             VAL[:, 1].unsqueeze(1).broadcast_to(grid), ALU.add), 3)
                step(lambda: v.max(BEST[:, 0:8], CAND))
                yield
                step(lambda: v.max_index(AT[:, 0:8], BEST[:, 0:8], CAND))
                step(lambda: v.match_replace(REST[:, 0, :], BEST[:, 0:8], CAND, NEG), 2)
                yield
                step(lambda: v.max(BEST[:, 8:16], REST[:, 0, :]))
                step(lambda: v.max_index(AT[:, 8:16], BEST[:, 8:16], REST[:, 0, :]))
                yield
                step(lambda: v.tensor_scalar(POS[:, 0], AT, 4, None, ALU.logical_shift_right))
                step(lambda: v.tensor_scalar(POS[:, 1], AT, TOPK - 1, None, ALU.bitwise_and), 2)
                io = iota16[:].unsqueeze(1).broadcast_to(grid)
                yield
                step(lambda: v.tensor_tensor(square(ONEHOT[:, 0]), POS[:, 0].unsqueeze(2).broadcast_to(grid), io, ALU.is_equal), 2)
                step(lambda: v.tensor_tensor(square(ONEHOT[:, 1]), POS[:, 1].unsqueeze(2).broadcast_to(grid), io, ALU.is_equal), 2)
                yield
                for i in range(2):
                    step(lambda: v.tensor_tensor(square(ONEHOT[:, i]), square(ONEHOT[:, i]),
                                                 KEY[:, i].unsqueeze(1).broadcast_to(grid), ALU.mult), 2)
                yield
                step(lambda: v.tensor_reduce(KEYF, ONEHOT.rearrange("p i (a b) -> p i a b", a=TOPK), AX_X, ALU.add))
                step(lambda: v.scalar_tensor_tensor(IDX[:, e], KEYF[:, 0], float(NKEYS), KEYF[:, 1], ALU.mult, ALU.add))
                yield
                step(lambda: v.tensor_scalar(CURU[:, e, :], IDX[:, e], float(layer * NEXP), None, ALU.add))
                step(lambda: v.tensor_tensor(GATE[:, e], BEST, BEST[:, 0:1].broadcast_to([P, TOPK]), ALU.subtract), 2)
                assert state["j"] == SEL_IDX
                yield
                v.wait_ge(s_gexp, u + 1)
                v.sem_inc(s_selgo, 1)
                step(lambda: v.tensor_reduce(gsm[:, 0, 0:1], GATE[:, e], AX_X, ALU.add))
                step(lambda: v.reciprocal(gsm[:, 1, 0:1], gsm[:, 0, 0:1]))
                step(lambda: v.tensor_scalar(GATE[:, e], GATE[:, e], gsm[:, 1, 0:1], None, ALU.mult))
                assert state["j"] == NSEL

            def experts(layer):
                u0 = layer * UNITS
                norm(2 * layer + 1)
                hs = H[:, :, NP_TOK:TOK].unsqueeze(2).broadcast_to([P, DC, 4, NS_TOK])
                V.do(v.tensor_copy(HS4.rearrange("p c (g t) -> p c g t", g=4), hs), s_hs4)
                v.wait_ge(s_q, 16 * (layer + 1))
                V.sync()
                V.chain(v.memset(QP, 0.0))
                for g in range(4):
                    V.do(v.tensor_copy(QP[:, 4 * g:4 * g + 4, 32 * g:32 * g + 32], Q[:, 4 * g:4 * g + 4, NP_TOK:TOK]))
                V.sync()
                v.sem_inc(s_qp, 1)
                v.wait_ge(s_crow, 32)
                V.chain(v.memset(OACC, 0.0))
                for e in range(2):
                    for _ in choose(u0 + e, e, layer):
                        pass
                u0 = layer * UNITS
                for j in range(3, 6):
                    n = GROUP[f"ht{layer}"] + j
                    v.wait_ge(bank_free[n % BANKS], n // BANKS + 1)

                def v_indices(e):
                    v.tensor_scalar(CURV[:, e, :], IDX[:, e], float(layer * NEXP), None, ALU.add).then_inc(s_vidx, 1)

                v.wait_ge(s_sel, (u0 + 2) * NSEL)
                v_indices(0)

                def z_of(u, k, e, h):
                    v.wait_ge(u_land[k % RING], u * 32 + 16 * (k // RING + 1))
                    v.scalar_tensor_tensor(RU[:, k % RING, :], RU[:, k % RING, :], 1.0, h, ALU.mult, ALU.mult,
                                           accum_out=ZB[:, e, k:k + 1]).then_inc(s_z, 1)

                for k in range(TOPK):
                    z_of(u0, k, 0, HTOK[:, 0, :])

                def unit(u, lu, e, last):
                    chosen = choose(u + 2, e, layer) if last == 0 else iter(())
                    if last < 2:
                        for k in range(TOPK):
                            if k == 2:
                                coef(u, e)
                            if k == 8:
                                v.wait_ge(s_sel, u * NSEL + 2 * NSEL)
                                v.wait_ge(v_free, u * 16 + RING)
                                v_indices(1 - e)
                            z_of(u + 1, k, 1 - e, at(HTOK, (lu + 1) // 8))
                            if k >= 2:
                                next(chosen, None)
                    else:
                        coef(u, e)
                    for _ in chosen:
                        pass
                    v.wait_ge(v_free, u * 16 + (16 + RING))
                    v.wait_ge(acc_free, u + 2)
                    oa = at(OACC, lu // 8)
                    v.tensor_tensor(oa, oa, ps[:, 4 + 2 * e:6 + 2 * e, :].rearrange("p b n -> p (b n)"), ALU.add).then_inc(acc_free, 1)

                def coef(u, e):
                    v.wait_ge(s_sel, u * NSEL + NSEL)
                    v.wait_ge(s_gelu, u + 1)
                    v.tensor_tensor(CF[:, e, :], GL[:, e, :], GATE[:, e], ALU.mult).then_inc(s_coef, 1)

                with v.Fori(0, UNITS // 2 - 1) as i:
                    for e in range(2):
                        unit(i * 2 + (u0 + e), i * 2 + e, e, 0)
                for e in range(2):
                    unit(u0 + UNITS - 2 + e, UNITS - 2 + e, e, 1 + e)
                v.wait_ge(acc_free, u0 + UNITS + 2)
                v.sem_inc(s_acc, 1)
                residual(f"res{layer}", 2 * layer + 1)

            def by_chunk(f):
                return f[:, :, 0:NP_TOK].rearrange("p c (q t) -> p c q t", t=CHUNK)

            def rwkv():
                v.wait_ge(s_const, 2)
                V.do(v.tensor_copy(TOKM[NS_TOK:2 * NS_TOK], TOKM[0:NS_TOK]))
                v.wait_ge(s_hp, 3 * DC)
                sh = H[:, :, NP_TOK:TOK].rearrange("p c (b t) -> p c b t", b=NSEQ)
                V.do(v.tensor_copy(COUT[:, :, 0:1], H[:, :, NP_TOK - 1:NP_TOK]))
                V.do(v.tensor_copy(COUT[:, :, 1:NCOND], sh[:, :, :, NSTEP - 1]))
                V.sync()
                v.sem_inc(s_sh, 1)
                sx = sample(XX)
                V.do(v.tensor_tensor(XX[:, :, 1:NP_TOK], H[:, :, 0:NP_TOK - 1], H[:, :, 1:NP_TOK], ALU.subtract))
                V.do(v.tensor_scalar(XX[:, :, 0:1], H[:, :, 0:1], -1.0, None, ALU.mult))
                V.do(v.tensor_tensor(sx[:, :, :, 1:NSTEP], sh[:, :, :, 0:NSTEP - 1], sh[:, :, :, 1:NSTEP], ALU.subtract))
                V.do(v.tensor_tensor(sx[:, :, :, 0], CT[:, :, CR_SHIFT:CR_SHIFT + NSEQ], sh[:, :, :, 0], ALU.subtract))
                V.sync()
                for i, which in enumerate((0, 2, 3, 1, 4, 5)):
                    if i >= 2:
                        last = [GROUP["rp"] + DC, GROUP["kp"] + DC, GROUP["vp"] + DC, GROUP["lm"] + 1][i - 2]
                        v.wait_ge(bank_ready, last)
                    if i == 1:
                        v.wait_ge(s_shr, 32)
                    for c in range(DC):
                        V.do(v.scalar_tensor_tensor((XI0, XI1)[i % 2][:, c, :], XX[:, c, :], col("rwkv_mix", 8 * which + c),
                                                    H[:, c, :], ALU.mult, ALU.add))
                    V.sync()
                    v.sem_inc(s_xi, 1)
                V.do(v.tensor_scalar(OMKA[:], cols("rwkv_k_a", DC), -1.0, 1.0, ALU.mult, ALU.add))
                V.sync()
                v.wait_ge(s_sg, 1)
                for c in range(DC):
                    V.do(v.tensor_scalar(AF[:, c, :], KF[:, c, :], col("rwkv_k_k", c), None, ALU.mult))
                V.sync()
                v.sem_inc(s_kk, 1)
                for c in range(DC):
                    V.do(v.tensor_scalar(XX[:, c, :], BF[:, c, :], col("rwkv_k_a", c), OMKA[:, c:c + 1], ALU.mult, ALU.add))
                V.sync()
                V.chain(v.tensor_tensor(KF, KF, XX, ALU.mult))
                for c in range(DC):
                    o, free = take("kn", c)
                    V.do(v.tensor_scalar(XI0[:, c, :], o[:, 0:TOK], 1e-24, None, ALU.max))
                    free_bank(free)
                v.sem_inc(s_kkn, 1)
                for c in range(DC):
                    V.do(v.scalar_tensor_tensor(XI1[:, c, :], RF[:, c, :], col("rwkv_r_k", c), KF[:, c, :], ALU.mult, ALU.mult))
                V.sync()
                v.sem_inc(s_rk, 1)
                for c in range(DC):
                    o, free = take("bn", c)
                    V.do(v.tensor_tensor(BON[:, c, :], o[:, 0:TOK], VF[:, c, :], ALU.mult))
                    free_bank(free)
                v.wait_ge(s_kkr, 1)
                V.chain(v.reciprocal(XI0, XI0))
                V.chain(v.tensor_tensor(AF, AF, XI0, ALU.mult))
                V.do(v.tensor_tensor(BF, BF, AF, ALU.mult))
                V.sync()
                V.chain(v.tensor_scalar(LW, LW, DECAY, None, ALU.mult))
                for c in range(DC):
                    V.do(v.tensor_tensor_scan(XX[:, c, :], SCM[:], LW[:, c, :], 0.0, ALU.mult, ALU.add))
                V.sync()
                mid = CHUNK // 2 - 1
                cc = by_chunk(XX)
                V.do(v.tensor_tensor(by_chunk(XI0), cc, cc[:, :, :, mid:mid + 1].broadcast_to([P, DC, NQ, CHUNK]), ALU.subtract))
                V.do(v.tensor_copy(XI0[:, :, NP_TOK:TOK], XX[:, :, NP_TOK:TOK]))
                V.do(v.tensor_copy(EC[:], sample(XX)[:, :, :, NSTEP - 1]))
                V.chain(v.tensor_tensor(FE[:], cc[:, :, :, CHUNK - 1], cc[:, :, :, mid], ALU.subtract))
                V.do(v.tensor_tensor(FE[:, :, 0:NQ - 1], FE[:, :, 0:NQ - 1], cc[:, :, 1:NQ, mid], ALU.add))
                V.do(v.tensor_tensor(LW, XI0, LW, ALU.subtract))
                V.sync()
                v.sem_inc(s_dc, 1)
                v.wait_ge(s_ex, 3)
                V.chain(v.tensor_tensor(RF, RF, XI1, ALU.mult))
                v.sem_inc(s_exu, 1)
                v.wait_ge(s_ex, 4)
                V.do(v.tensor_tensor(KF, KF, XI1, ALU.mult))
                V.chain(v.tensor_tensor(BF, BF, XI1, ALU.mult))
                v.sem_inc(s_exu, 1)
                v.wait_ge(s_ex, 5)
                V.do(v.scalar_tensor_tensor(AF, AF, -1.0, LW, ALU.mult, ALU.mult))
                ecb = EC[:].unsqueeze(3).broadcast_to([P, DC, NSEQ, NSTEP])
                for i, f in enumerate((BF, KF)):
                    V.do(v.tensor_tensor(BBS[:, i].rearrange("p c (b t) -> p c b t", b=NSEQ), sample(f), ecb, ALU.mult))
                V.sync()
                v.sem_inc(s_wkv, 1)
                V.do(v.memset(SB, 0.0))
                V.do(v.memset(RAW, 0.0))
                V.sync()
                v.sem_inc(s_wkv, 1)
                v.sem_inc(s_raw0, 1)
                for tile in range(3):
                    n = P if tile < 2 else NS_TOK
                    nm = f"nm{tile}"
                    steps = NM_STEPS if tile < 2 else NM_STEPS_S

                    def wide(m):
                        return m[0:n].unsqueeze(1).broadcast_to([n, 4, n])

                    for bp in range(2):
                        for step in range(steps):
                            for b in range(2):
                                if step in ((5, 6, 9, 10, 13, 16, 19) if tile < 2 else (5,)):
                                    continue
                                o, free = take(nm, (bp * steps + step) * 2 + b)
                                o = o[0:n, 0:4 * n].rearrange("p (h t) -> p h t", h=4)
                                h0 = slot(2 * 4 * bp + b)
                                gg = [(GG[0:n, i] if tile < 2 else GS[i][0:n])[:, h0:h0 + 4, :] for i in range(4)]
                                T = NT[0:n, b, :, :, 0:n]
                                G = gg[3]
                                if step == 0:
                                    V.chain(v.tensor_tensor(T[:, 1], o, wide(M8U if tile < 2 else M4U), ALU.mult))
                                    V.chain(v.tensor_tensor(G, T[:, 1], wide(ident[:, 0:n]), ALU.add))
                                elif step == 1:
                                    V.do(v.tensor_tensor(T[:, 0], o, wide(M8A if tile < 2 else M4A), ALU.mult))
                                    if tile < 2:
                                        for i, m in enumerate((O8A, O16A, O32A)):
                                            V.do(v.tensor_tensor(T[:, 5 + i], o, wide(m), ALU.mult))
                                        V.sync()
                                        V.do(v.tensor_tensor(T[:, 4], T[:, 0], wide(ident[:]), ALU.add))
                                elif step < 5:
                                    mask = ((S64U, I64U, I64U) if tile < 2 else (M4U, I4U, I4U))[step - 2]
                                    V.do(v.tensor_tensor(gg[step - 2], o, wide(mask), ALU.mult))
                                else:
                                    dst = T[:, 4] if step in (8, 12, 15, 18) else G
                                    V.do(v.tensor_tensor(dst, dst, o, ALU.add))
                                free_bank(free)
                    if tile < 2:
                        for ch in range(2):
                            for q in range(2):
                                o, free = take(f"sq{tile}", 8 * ch + 6 + q)
                                for j in range(4):
                                    c = 4 * q + j
                                    V.do(v.scalar_tensor_tensor(SB[:, c, :], o[:, j * P:(j + 1) * P], FE[:, c, 2 * tile + ch:2 * tile + ch + 1],
                                                                BLK, ALU.mult, ALU.mult))
                                free_bank(free)
                        v.wait_ge(bank_free[(GROUP[f"sq{tile}"] + 12) % BANKS], (GROUP[f"sq{tile}"] + 12) // BANKS + 1)
                        v.wait_ge(bank_free[(GROUP[f"sq{tile}"] + 13) % BANKS], (GROUP[f"sq{tile}"] + 13) // BANKS + 1)
                        if tile == 1:
                            v.wait_ge(bank_ready, GROUP["pso"] + 2)
                    else:
                        tok = TOKM[0:2 * n].unsqueeze(2).broadcast_to([2 * n, NSEQ, P])

                        def masked(c):
                            for i, f in enumerate((AF, RF)):
                                V.do(v.tensor_tensor(ART[:, c % 2, :, i, :], f[:, c, NP_TOK:TOK].unsqueeze(1).broadcast_to([P, NSEQ, NS_TOK]),
                                                     SEQM[:], ALU.mult))
                            V.sync()
                            v.sem_inc(s_atm, 1)

                        v.wait_ge(s_v2, 1)
                        for c in range(2):
                            masked(c)
                        for kind, c in SQ2:
                            if kind[:4] in ("turn", "out0", "out1"):
                                continue
                            o, free = take("sq2", SQ2.index((kind, c)))
                            pair = slice(c * P, (c + 1) * P)
                            if kind == "right":
                                V.do(v.tensor_copy(RHS[0:n], o[0:n, 0:P]))
                                V.do(v.tensor_copy(YR[0:n, pair], o[n:2 * n, 0:P]))
                                free_bank(free)
                                if 0 < c < DC - 1:
                                    masked(c + 1)
                            elif kind == "sa":
                                V.do(v.tensor_copy(SAV[0:n, pair], o[0:n, 0:P]))
                                free_bank(free)
                                V.chain(v.tensor_tensor(SAVM[0:2 * n], SAV[0:2 * n, pair].unsqueeze(1).broadcast_to([2 * n, NSEQ, P]),
                                                        tok, ALU.mult))
                                v.sem_inc(s_sam, 1)
                                for k in ("turn0", "turn1"):
                                    nt = GROUP["sq2"] + SQ2.index((k, c))
                                    v.wait_ge(bank_free[nt % BANKS], nt // BANKS + 1)
                                V.chain(v.tensor_tensor(NEW[:, c % 2], SS[:, c % 2], EC[:, c, :].unsqueeze(2).broadcast_to([P, NSEQ, P]),
                                                        ALU.mult))
                                v.sem_inc(s_kept, 1)
                            elif kind == "y":
                                V.do(v.tensor_tensor(YR[0:n, pair], YR[0:n, pair], o[0:n, 0:P], ALU.add))
                                free_bank(free)
                            else:
                                half = int(kind[-1])
                                dst = NEW[:, c % 2, 4 * half:4 * half + 4, :]
                                V.do(v.tensor_tensor(dst, dst, o.rearrange("p (s n) -> p s n", s=4), ALU.add))
                                free_bank(free)
                    y3 = YR[0:n].rearrange("p (h i) -> p h i", h=WHEADS)
                    k3 = KTK[0:n].rearrange("p (h i) -> p h i", h=WHEADS)
                    wide16 = lambda s: s.unsqueeze(2).broadcast_to([n, WHEADS, HS])
                    V.chain(v.tensor_reduce(gst[0:n, 0, :], y3, AX_X, ALU.add))
                    V.chain(v.tensor_scalar(gst[0:n, 0, :], gst[0:n, 0, :], -1.0 / HS, None, ALU.mult))
                    V.chain(v.tensor_tensor(y3, y3, wide16(gst[0:n, 0, :]), ALU.add))
                    V.chain(v.tensor_tensor(k3, y3, y3, ALU.mult))
                    V.chain(v.tensor_reduce(gst[0:n, 1, :], k3, AX_X, ALU.add))
                    V.chain(v.tensor_scalar(gst[0:n, 1, :], gst[0:n, 1, :], 1.0 / HS, GN_EPS, ALU.mult, ALU.add), s_gn)
                    v.wait_ge(s_gnr, tile + 1)
                    V.chain(v.reciprocal(gst[0:n, 2, :], gst[0:n, 1, :]))
                    V.chain(v.tensor_tensor(y3, y3, wide16(gst[0:n, 2, :]), ALU.mult))
                    v.sem_inc(s_yn, 1)
                    for q in range(2):
                        o, free = take(f"gn{tile}", q)
                        for j in range(4):
                            c = 4 * q + j
                            V.do(v.tensor_scalar(H[:, c, tile * P:tile * P + n], o[:, j * n:(j + 1) * n], col("rwkv_lnw", c),
                                                 col("rwkv_lnb", c), ALU.mult, ALU.add))
                        free_bank(free)
                gains("adb", 8, (3,))
                V.chain(v.tensor_tensor(H[:], H[:], BON, ALU.add))
                V.chain(v.tensor_tensor(H[:], H[:], GF, ALU.mult))
                v.sem_inc(s_wy, 1)
                residual("wo", 2)

            experts(0)
            norm(2)
            rwkv()
            v.wait_ge(s_stout[0], 16 * DC)
            v.wait_ge(s_stout[1], 16 * DC)
            experts(1)
            norm(4)

        @block.gpsimd
        def _(pool):
            G = Steps(pool, pool_step)
            G.chain(pool.memset(ident[:], 0.0))
            G.chain(pool.affine_select(out=ident[:], in_=ident[:], compare_op=ALU.not_equal, fill=1.0, base=0,
                                       pattern=[[-1, P]], channel_multiplier=1))
            G.do(pool.memset(ones[:], 1.0))
            G.do(pool.iota(iota16[:], pattern=[[1, TOPK]], base=0, channel_multiplier=0, allow_small_or_imprecise_dtypes=True))
            def mask(dst, n, block, tri, inner=None):
                def keep(v, pattern, base, mult, op=ALU.is_ge):
                    G.chain(pool.affine_select(out=v, in_=v, compare_op=op, fill=0.0, base=base, pattern=pattern,
                                               channel_multiplier=mult))

                G.chain(pool.memset(dst, 1.0))
                v3 = dst.rearrange("p (b r) -> p b r", r=block)
                keep(v3, [[-block, n // block], [0, block]], 0, 1)
                keep(v3, [[block, n // block], [0, block]], block - 1, -1)
                if tri in ("u", "U"):
                    keep(dst, [[1, n]], -1 if tri == "u" else 0, -1)
                elif tri == "l":
                    keep(dst, [[-1, n]], -1, 1)
                if inner:
                    keep(dst.rearrange("p (b r) -> p b r", r=inner), [[-inner, n // inner], [0, inner]], -inner, 1)

            G.sync()
            pool.sem_inc(s_const, 1)
            mask(M8U, P, 8, "u")
            mask(M8A, P, 8, "l")
            mask(O8A, P, 16, "l", 8)
            mask(O16A, P, 32, "l", 16)
            mask(O32A, P, 64, "l", 32)
            mask(S64U, P, CHUNK, "u")
            mask(I64U, P, CHUNK, "U")
            mask(BLK, P, HS, None)
            mask(M4U, NS_TOK, NSTEP, "u")
            mask(M4A, NS_TOK, NSTEP, "l")
            mask(I4U, NS_TOK, NSTEP, "U")
            G.chain(pool.memset(SEQM[:], 1.0))
            for base, mult in ((0, 1), (NSTEP - 1, -1)):
                G.chain(pool.affine_select(out=SEQM[:], in_=SEQM[:], compare_op=ALU.is_ge, fill=0.0, base=base,
                                           pattern=[[-NSTEP * mult, NSEQ], [mult, NS_TOK]], channel_multiplier=0))
            G.chain(pool.memset(TOKM[:], 1.0))
            for base, mult in ((0, 1), (NSTEP - 1, -1)):
                G.chain(pool.affine_select(out=TOKM[:], in_=TOKM[:], compare_op=ALU.is_ge, fill=0.0, base=base,
                                           pattern=[[-NSTEP * mult, NSEQ]], channel_multiplier=mult))
            G.chain(pool.memset(SCM[:], 1.0))
            G.do(pool.memset(SCM[:, 0:NP_TOK].rearrange("p (q t) -> p q t", t=CHUNK)[:, :, 0:1], 0.0))
            G.do(pool.memset(SCM[:, NP_TOK:].rearrange("p (q t) -> p q t", t=NSTEP)[:, :, 0:1], 0.0))
            G.sync()
            pool.sem_inc(s_const, 1)
            u_tab = a["peer_u"].rearrange("l e d -> (l e) d")
            v_tab = a["peer_v"].rearrange("l e d -> (l e) d")

            def gather(ring, tab, idx, k, landed):
                pool.indirect_dma_start(ring[:, k % RING, :], None, tab,
                                        bass.IndirectOffsetOnAxis(ap=idx[:, k:k + 1], axis=0)).then_inc(landed[k % RING], 16)

            def experts(layer):
                u0 = layer * UNITS

                def get_u(u, k, e):
                    if k == 0:
                        pool.wait_ge(s_sel, u * NSEL + SEL_IDX)
                    if k >= RING or not isinstance(u, int) or u > 0:
                        pool.wait_ge(s_z, u * 16 + (k - RING + 1))
                    pool.sem_inc(s_go, 1)
                    gather(RU, u_tab, CURU[:, e, :], k, u_land)

                def get_v(u, k, e):
                    if k == 0:
                        pool.wait_ge(s_vidx, u + 1)
                    pool.wait_ge(v_free, u * 16 + (k + 1))
                    pool.sem_inc(s_go, 1)
                    gather(RVV, v_tab, CURV[:, e, :], k, v_land)

                pool.wait_ge(bank_ready, GROUP[f"ht{layer}"] + 6)
                for k in range(TOPK):
                    get_u(u0, k, 0)
                with pool.Fori(0, UNITS // 2 - 1) as i:
                    for e in range(2):
                        for k in range(TOPK):
                            get_v(i * 2 + (u0 + e), k, e)
                            get_u(i * 2 + (u0 + e + 1), k, 1 - e)
                for k in range(TOPK):
                    get_v(u0 + UNITS - 2, k, 0)
                    get_u(u0 + UNITS - 1, k, 1)
                for k in range(TOPK):
                    get_v(u0 + UNITS - 1, k, 1)

            experts(0)
            experts(1)


_INS = ['x_prompt', 'x_sample', 'state_conv', 'state_shift', 'state_wkv', 'c_prompt', 'c_sample', 'w_ada', 'b_ada',
        'g_mix', 'g_ffn', 'g_final', 'conv_w_in', 'conv_k', 'conv_w_out', 'rwkv_mix', 'rwkv_wr', 'rwkv_wk', 'rwkv_wv',
        'rwkv_wo', 'rwkv_w0', 'rwkv_w1', 'rwkv_w2', 'rwkv_a0', 'rwkv_a1', 'rwkv_a2', 'rwkv_g1', 'rwkv_g2', 'rwkv_k_k',
        'rwkv_k_a', 'rwkv_r_k', 'rwkv_lnw', 'rwkv_lnb', 'peer_wq', 'peer_k1', 'peer_k2', 'peer_u', 'peer_v']
_OUTS = [(1, 256, 1024), (8, 4, 1024), (1, 1, 2, 1024), (1, 1, 1024), (1, 1, 16, 64, 64), (1, 8, 2, 1024),
         (1, 8, 1024), (1, 8, 16, 64, 64)]


def kernel(**inputs):
    import numpy as _np
    import concourse.bacc as _bacc
    from concourse import mybir as _mybir
    from concourse.bass_utils import run_bass_kernel_spmd as _run

    nc = _bacc.Bacc("TRN2", target_bir_lowering=False, num_devices=1)
    arrays, aps, outs = {}, {}, []
    for name in _INS:
        x = _np.ascontiguousarray(inputs[name])
        arrays[f"in_{name}"] = x
        aps[name] = nc.dram_tensor(f"in_{name}", x.shape, _mybir.dt.from_np(x.dtype), kind="ExternalInput").ap()
    for i, shape in enumerate(_OUTS):
        outs.append(nc.dram_tensor(f"out_{i}", shape, _mybir.dt.float32, kind="ExternalOutput").ap())
    build(nc, aps, outs)
    r = _run(nc, [arrays], core_ids=[0])
    return tuple(r.results[0][f"out_{i}"] for i in range(len(_OUTS)))
```

```python
from contextlib import ExitStack

import numpy as np
import concourse.bass as bass
from concourse import mybir

ALU = mybir.AluOpType
ACT = mybir.ActivationFunctionType
F32 = mybir.dt.float32
U32 = mybir.dt.uint32
AX_X = mybir.AxisListType.X

P = 128
D = 1024
DC = D // P
NP_TOK = 256
NSEQ, NSTEP = 8, 4
NS_TOK = NSEQ * NSTEP
TOK = NP_TOK + NS_TOK
NCOND = 1 + NSEQ
DEPTH = 2
EPS = 1e-6
HEADS = 8
NKEYS = 128
NEXP = NKEYS * NKEYS
TOPK = 16
UNITS = 18
RING = 8
NDIAG = 4
WRING = 4
BANKS = 4
NEG = -3.0e38
GEXP_AT = (7, 11)
NSEL = 29
SEL_IDX = 26
GN_EPS = 64e-5
WHEADS, HS = 16, 64
DECAY = -float(np.exp(-0.5))
CHUNK = 64
NQ = NP_TOK // CHUNK
LW_, LA_, LG_ = 64, 64, 128

ROWS = {}


def _rows():
    at = 0
    for name, n in (("g_mix", 16), ("g_ffn", 16), ("g_final", 8), ("conv_k", 24), ("rwkv_mix", 48),
                    ("rwkv_w0", 8), ("rwkv_a0", 8), ("rwkv_k_k", 8), ("rwkv_k_a", 8), ("rwkv_r_k", 8),
                    ("rwkv_lnw", 8), ("rwkv_lnb", 8), ("b_ada0", 48), ("pad", 40), ("b_ada1", 48)):
        ROWS[name] = at
        at += n
    return at


NROWS = _rows()
PAR_ROWS = (P, ROWS["b_ada0"] + 48 - P, 48)
CR_COND, CR_CONV, CR_SHIFT, CR_N = 0, NCOND, NCOND + 2 * NSEQ, NCOND + 3 * NSEQ

ADA_PARTS = {"ad0": [(0, j) for j in range(6)], "ad1": [(0, j) for j in range(6, 10)] + [(1, j) for j in range(4)],
             "ad2": [(0, 10)], "ad3": [(0, 11)], "ad4": [(1, 4), (1, 5)], "ad5": [(1, 6)], "ad6": [(1, 7)],
             "ad7": [(1, j) for j in range(8, 12)]}


def ada_stage(name):
    return [(name, 2 * len(ADA_PARTS[name]))]


STAGES = [("crow", 1), ("x", DC), ("par", 1), ] + ada_stage("ad0") + [("nrm0", 1)] + ada_stage("ad1")
STAGES += [("cin", 24), ("kt0", 4)] + ada_stage("ad2") + [("cout", DC), ("cst", 2)]
STAGES += [("nrm1", 1)] + ada_stage("ad3") + [("hf0", 2), ("qa0", 4), ("se0", 1), ("qb0", 12), ("sc0", 9), ("ht0", 4), ("res0", DC)]
STAGES += [("nrm2", 1)] + ada_stage("ad4") + [("rp", DC), ("sst", 2), ("kp", DC), ("vp", DC), ("lm", 3), ("l2", 24)]
STAGES += ada_stage("ad5") + [("kn", DC)] + ada_stage("ad6") + [("bn", DC)] + ada_stage("ad7")
NM_STEPS, NM_STEPS_S = 21, 7
for _t in range(2):
    STAGES += [(f"tm{_t}", 6), (f"nm{_t}a", 2 * NM_STEPS)] + [("gn0", 2)] * (_t == 1)
    STAGES += [(f"nm{_t}b", 2 * NM_STEPS), (f"sq{_t}", 16)] + [("pso", 2)] * (_t == 1)
STAGES += [("tm2", 6), ("nm2a", 2 * NM_STEPS_S), ("gn1", 2), ("nm2b", 2 * NM_STEPS_S), ("sq2", 9 * DC), ("gn2", 2), ("wo", DC)]
STAGES += [("kt1", 4), ("nrm3", 1), ("hf1", 2), ("qa1", 4), ("se1", 1), ("qb1", 12), ("sc1", 9), ("ht1", 4), ("res1", DC)]
STAGES += [("nrm4", 1), ("fin", 6)]

SQ2 = []
for _c in range(-1, DC + 1):
    SQ2 += [("turn0", _c + 1), ("turn1", _c + 1), ("sa", _c), ("out0", _c - 1), ("out1", _c - 1),
            ("right", _c + 1), ("y", _c), ("new0", _c), ("new1", _c)]
SQ2 = [g for g in SQ2 if 0 <= g[1] < DC]
GROUP = {}
_n = 0
for _name, _count in STAGES:
    GROUP[_name] = _n
    _n += _count


class Steps:

    def __init__(self, eng, sem):
        self.eng, self.sem, self.counts, self.last = eng, sem, {}, None

    def do(self, ins, sem=None):
        sem = sem or self.sem
        ins.then_inc(sem, 1)
        self.counts[sem.name] = self.counts.get(sem.name, 0) + 1
        self.last = (sem, self.counts[sem.name])
        return ins

    def sync(self):
        if self.last:
            self.eng.wait_ge(*self.last)

    def chain(self, ins, sem=None):
        self.do(ins, sem)
        self.sync()


def build(nc, a, out):
    with ExitStack() as ctx:
        def sb(name, shape, dt=F32):
            return ctx.enter_context(nc.sbuf_tensor(name, [P] + list(shape), dt))

        def sem(name):
            return ctx.enter_context(nc.semaphore(name))

        ps = ctx.enter_context(nc.psum_tensor("ps", [P, 8, 512], F32))
        X = sb("X", [DC, TOK])
        H = sb("H", [DC, TOK])
        PAR = sb("PAR", [3 * P])
        CT = sb("CT", [DC, CR_N])
        ADA = sb("ADA", [DEPTH, 48, NCOND])
        GA = sb("GA", [2 * DEPTH, DC, NCOND])
        ident = sb("ident", [P])
        ones = sb("ones", [P])
        sel = sb("sel", [NS_TOK])
        iota16 = sb("iota16", [TOPK])
        rms = sb("rms", [TOK])
        rstd = sb("rstd", [TOK])
        tmpS = sb("tmpS", [2, NS_TOK])
        W = sb("W", [WRING, DC, 512])
        N_RV, N_ROWS, N_SEL = 2 * RING * D, 3 * D, 2880
        ARENA = sb("ARENA", [N_RV + 2 * N_ROWS + N_SEL])
        RV = ARENA[:, 0:N_RV]
        HTOK = ARENA[:, N_RV:N_RV + N_ROWS].rearrange("p (a d) -> p a d", a=3)
        OACC = ARENA[:, N_RV + N_ROWS:N_RV + 2 * N_ROWS].rearrange("p (a d) -> p a d", a=3)
        CURU = sb("CURU", [2, TOPK], U32)
        CURV = sb("CURV", [2, TOPK], U32)
        ZB = sb("ZB", [2, TOPK])
        GL = sb("GL", [2, TOPK])
        CF = sb("CF", [2, TOPK])
        DG = sb("DG", [NDIAG, P])
        scr = sb("scr", [2, 256])
        gsm = sb("gsm", [2, 2])
        COUT = sb("COUT", [DC, 18])

        rings = RV.rearrange("p (r s d) -> p r s d", r=2, s=RING)
        RU, RVV = rings[:, 0], rings[:, 1]

        def carve(off, shape, dt=F32):
            n = int(np.prod(shape))
            v = ARENA[:, off:off + n]
            if dt is not F32:
                v = v.bitcast(dt)
            names = " ".join("abcd"[:len(shape)])
            return v.rearrange(f"p ({names}) -> p {names}", **{"abcd"[i]: s for i, s in enumerate(shape)})

        PR = carve(0, [3, P])
        XR = carve(384, [3, D])
        CRAW = carve(384 + 3 * D, [D])
        SQ = carve(0, [DC, TOK])
        HN = carve(DC * TOK, [DC, TOK])
        BG = carve(0, [DC, TOK])
        CG = carve(DC * TOK, [DC, TOK])
        UHW = NP_TOK + 2 + NSEQ * 6
        UH = carve(2 * DC * TOK, [DC, UHW])
        CV = carve(2 * DC * TOK + DC * UHW, [DC, TOK])
        CS = carve(2 * DC * TOK + DC * UHW + DC * TOK, [DC * NS_TOK])
        CROW = carve(N_RV + N_ROWS, [D])
        KR = [carve(off, [2, HEADS, P]) for off in (RING * D + 2560, RING * D + 512)]
        Q = carve(RING * D, [16, TOK])
        KT = carve(RING * D + 16 * TOK, [2, HEADS, NKEYS])
        QP = carve(N_RV + N_ROWS, [16, P])
        HS4 = carve(N_RV + N_ROWS + 16 * P, [DC, P])
        CROW2 = carve(4 * DC * TOK, [D])
        YT = carve(2 * DC * TOK, [3, D])

        sel0 = N_RV + 2 * N_ROWS
        SCUR = carve(sel0, [2, 2, NKEYS])
        CAND = carve(sel0 + 512, [256])
        REST = carve(sel0 + 768, [2, 256])
        ONEHOT = carve(sel0 + 1280, [2, 256])
        sm = carve(sel0 + 1792, [16, TOPK])
        VAL, KEY, BEST, AT = sm[:, 0:2], sm[:, 2:4].bitcast(U32), sm[:, 4], sm[:, 5].bitcast(U32)
        POS = sm[:, 6:8].bitcast(U32)
        KEYF, IDX, GATE = sm[:, 8:10], sm[:, 10:12], sm[:, 12:14]
        SCALL = W[:].rearrange("p s c m -> p (s c m)")[:, 8192:8192 + UNITS * 256].rearrange("p (u n) -> p u n", u=UNITS)
        ADR = (scr[:].rearrange("p a b -> p (a b)"), DG[:].rearrange("p a b -> p (a b)"))

        FM = DC * TOK
        RF, KF, VF, BF, AF, GF, BON, LW, XX, XI0, XI1 = (carve(i * FM, [DC, TOK]) for i in range(11))
        rest = 7 * FM
        VT, BT, KTK = (carve(rest + i * D, [D]) for i in range(3))
        YR = carve(rest + 3 * D, [D])
        SB = carve(rest + 4 * D, [DC, P])
        SB2 = (scr[:].rearrange("p a b -> p (a b)").rearrange("p (c n) -> p c n", c=4), DG[:])
        RH = carve(rest + 5 * D, [DC, P])
        SA = carve(rest + 6 * D, [DC, P])
        RAW = carve(rest + 7 * D, [2, NSEQ, P])
        OUTB = carve(rest + 5 * D, [2, NSEQ, P])
        PSO = carve(rest + 5 * D, [DC, P])
        Wf = W[:].rearrange("p s c m -> p (s c m)")
        NT = Wf[:, 0:8192].rearrange("p (b k h t) -> p b k h t", b=2, k=8, h=4)
        GG = Wf[:, 8192:16384].rearrange("p (i h t) -> p i h t", i=4, h=WHEADS)
        gs = Wf[:, 8192:16384]
        GKV = gs[:, 0:1024].rearrange("p (h r t) -> p h r t", h=WHEADS, r=2)
        G13 = gs[:, 1024:2048].rearrange("p (r h t) -> p r h t", r=2, h=WHEADS)
        GS = (GKV[:, :, 0], G13[:, 0], GKV[:, :, 1], G13[:, 1])
        SS = gs[:, 2048:4096].rearrange("p (e s n) -> p e s n", e=2, s=NSEQ)
        NEW = gs[:, 4096:6144].rearrange("p (e s n) -> p e s n", e=2, s=NSEQ)
        ART = gs[:, 6144:7168].rearrange("p (e s r t) -> p e s r t", e=2, s=NSEQ, r=2)
        RHS = gs[:, 7168:7168 + P]
        SAV = KTK
        SAVM = SB.rearrange("p c n -> p (c n)").rearrange("p (s n) -> p s n", s=NSEQ)
        L1 = W[:, 0].rearrange("p c m -> p (c m)")[:, 0:2048].rearrange("p (c m) -> p c m", c=DC)
        L2 = W[:, 1].rearrange("p c m -> p (c m)")[:, 0:3072].rearrange("p (c m) -> p c m", c=3)
        LM = W[:, 1].rearrange("p c m -> p (c m)")[:, 3072:3072 + 3 * TOK].rearrange("p (c m) -> p c m", c=3)
        MASKS = sb("MASKS", [8, P])
        M8U, M8A, O8A, O16A, O32A, S64U, I64U, BLK = (MASKS[:, i] for i in range(8))
        MS = sb("MS", [3, NS_TOK])
        M4U, M4A, I4U = (MS[:, i] for i in range(3))
        SEQM = sb("SEQM", [NSEQ, NS_TOK])
        TOKM = sb("TOKM", [NSEQ])
        SCM = sb("SCM", [TOK])
        FE = sb("FE", [DC, NQ])
        EC = sb("EC", [DC, NSEQ])
        BBS = sb("BBS", [2, DC, NS_TOK])
        OMKA = sb("OMKA", [DC])
        gst = sb("gst", [3, WHEADS])

        s_sh, s_shr = sem("shift_columns_ready"), sem("shift_rows_out")
        s_xi, s_x0 = sem("mixed_ready"), sem("first_mixed_chunks_ready")
        s_sg = sem("decay_rate_gate_ready")
        s_kk, s_kksq, s_kkn, s_kkr = sem("kk_ready"), sem("kk_squares_ready"), sem("kk_norm_ready"), sem("kk_root_ready")
        s_rk = sem("rk_products_ready")
        s_dc, s_ex, s_exu = sem("decay_sums_ready"), sem("decay_exp_ready"), sem("decay_exp_used")
        s_wkv = sem("wkv_operands_ready")
        s_raw0, s_raw = sem("raw_zero"), [sem("raw_loaded0"), sem("raw_loaded1")]
        s_sq = sem("squares_ready")
        s_gn, s_gnr, s_yn = sem("gn_var_ready"), sem("gn_root_ready"), sem("y_normed")
        s_atm, s_sam, s_kept = sem("seq_masked_ready"), sem("sa_and_v_masked"), sem("states_decayed")
        s_v2 = sem("v_rows_again")
        s_stout = [sem("state_out0"), sem("state_out1")]
        s_wy = sem("mixer_rows_ready")

        s_par, s_cr, s_x, s_keys = sem("par_loaded"), sem("cond_rows_loaded"), sem("x_loaded"), sem("keys_loaded")
        s_const = sem("consts_ready")
        s_out = sem("outputs_written")
        w_load = [sem(f"weights_loaded{i}") for i in range(WRING)]
        bank_ready = sem("bank_ready")
        bank_free = [sem(f"bank_free{i}") for i in range(BANKS)]
        s_silu = sem("silu_ready")
        s_xready = sem("x_ready")
        s_ms, s_rms = sem("mean_square_ready"), sem("rms_ready")
        s_h = sem("h_ready")
        s_gates = sem("conv_gates_ready")
        s_cv = sem("conv_ready")
        s_cout = sem("conv_state_ready")
        s_crow = sem("conv_rows_ready")
        s_kt = sem("keys_turned")
        s_q = sem("queries_ready")
        s_qp = sem("sample_queries_ready")
        s_hp = sem("prompt_h_ready")
        s_hn = sem("normed_ready")
        s_hf = sem("final_h_ready")
        s_scur = sem("unit_scores_ready")
        s_sel, s_selgo = sem("selection_steps"), sem("selection_goes_on")
        s_actgo = sem("unit_copies_started")
        s_gexp = sem("gate_exp_ready")
        s_hs4 = sem("sample_h_repeated")
        s_vidx = sem("v_indices_ready")
        u_land = [sem(f"u_landed{i}") for i in range(RING)]
        v_land = [sem(f"v_landed{i}") for i in range(RING)]
        s_z = sem("z_done")
        s_gelu = sem("gelu_ready")
        s_coef = sem("coef_ready")
        s_diag = sem("diag_ready")
        v_free = sem("v_slots_free")
        acc_free = sem("acc_free")
        s_go = sem("gather_steps")
        s_acc = sem("expert_rows_ready")
        s_yt = sem("y_rows_ready")
        dve_step, pool_step = sem("dve_step"), sem("pool_step")

        tiles = []

        def weight_tiles(w, k, cols, group0, per):
            for j in range(cols // 512):
                tiles.append(([(None, w[:, j * 512:(j + 1) * 512].rearrange("(c p) m -> p c m", p=P))],
                              group0 + per * (j + 1) - 1))

        def ada_rows(j):
            return max(2 * j - 1, 0)

        def ada_cols(j, n):
            return 2 * j + 2 if j < n - 1 else 2 * n - 1

        def later_queries(layer):
            for j in range(1, 4):
                tiles[WT[f"q{layer}"] + j] = (tiles[WT[f"q{layer}"] + j][0], GROUP[f"qb{layer}"] + 4 * j - 1)

        WT = {}

        def ada_tiles(name):
            WT[name] = len(tiles)
            for i, (layer, j) in enumerate(ADA_PARTS[name]):
                weight_tiles(a["w_ada"][layer][:, j * 512:(j + 1) * 512], D, 512, GROUP[name] + ada_rows(i), 1)

        ada_tiles("ad0")
        ada_tiles("ad1")
        WT["cin"] = len(tiles)
        weight_tiles(a["conv_w_in"][0], D, 3 * D, GROUP["cin"], 4)
        ada_tiles("ad2")
        WT["cout"] = len(tiles)
        weight_tiles(a["conv_w_out"][0], D, D, GROUP["cout"], 4)
        ada_tiles("ad3")
        WT["q0"] = len(tiles)
        weight_tiles(a["peer_wq"][0], D, 2 * D, GROUP["qa0"], 4)
        later_queries(0)
        ada_tiles("ad4")
        for name in ("wr", "wk", "wv"):
            WT[name] = len(tiles)
            weight_tiles(a["rwkv_" + name][0], D, D, GROUP[name[1] + "p"], 4)
        WT["l1"] = len(tiles)
        tiles.append(([(lambda _: L1[:, :, 0:LW_], a["rwkv_w1"][0].rearrange("(c p) m -> p c m", p=P)),
                       (lambda _: L1[:, :, LW_:LW_ + LA_], a["rwkv_a1"][0].rearrange("(c p) m -> p c m", p=P)),
                       (lambda _: L1[:, :, LW_ + LA_:], a["rwkv_g1"][0].rearrange("(c p) m -> p c m", p=P))],
                      GROUP["lm"] + 2))
        WT["l2"] = len(tiles)
        tiles.append(([(lambda _: L2[0:LW_, 0, :], a["rwkv_w2"][0]), (lambda _: L2[0:LA_, 1, :], a["rwkv_a2"][0]),
                       (lambda _: L2[:, 2, :], a["rwkv_g2"][0])], GROUP["l2"] + 23))
        assert WT["wr"] % WRING == 2 and WT["l1"] % WRING == 0 and WT["l2"] % WRING == 1
        for name in ("ad5", "ad6", "ad7"):
            ada_tiles(name)
        WT["wo"] = len(tiles)
        weight_tiles(a["rwkv_wo"][0], D, D, GROUP["wo"], 4)
        WT["q1"] = len(tiles)
        weight_tiles(a["peer_wq"][1], D, 2 * D, GROUP["qa1"], 4)
        later_queries(1)
        load_val, _seen = [], [0] * WRING
        for t, (parts, _) in enumerate(tiles):
            _seen[t % WRING] += 16 * len(parts)
            load_val.append(_seen[t % WRING])

        def state_of(n, c):
            return SB[:, c, :] if n % 2 == 0 else SB2[c // 4][:, c % 4, :]

        def slot(h):
            return h % 2 * DC + h // 2

        block = ctx.enter_context(nc.Block())

        def col(name, i=0):
            return PAR[:, ROWS[name] + i:ROWS[name] + i + 1]

        def cols(name, n):
            return PAR[:, ROWS[name]:ROWS[name] + n]

        def shift_of(which):
            return ADA[:, which // 2, 24 * (which % 2):24 * (which % 2) + 8, :]

        def scale_of(which):
            return ADA[:, which // 2, 24 * (which % 2) + 8:24 * (which % 2) + 16, :]

        def gate_of(which):
            return ADA[:, which // 2, 24 * (which % 2) + 16:24 * (which % 2) + 24, :]

        def at(v, i):
            return v[:, bass.ds(i, 1), :].rearrange("p a n -> p (a n)")

        def per_step(v):
            v = v[:, :, 1:NCOND].unsqueeze(3)
            return v.broadcast_to([P, v.shape[1], NSEQ, NSTEP])

        def sample(v):
            return v[:, :, NP_TOK:TOK].rearrange("p c (b t) -> p c b t", b=NSEQ)

        @block.sync
        def _(sp):
            def rows_in(name, src, n):
                at = ROWS[name]
                sp.dma_start(PR[at % P:at % P + n, at // P, :], src).then_inc(s_par, 16)

            def load_tile(t):
                for dst, src in tiles[t][0]:
                    sp.dma_start(W[:, t % WRING] if dst is None else dst(t % WRING), src).then_inc(w_load[t % WRING], 16)

            load_tile(0)
            rows_in("g_mix", a["g_mix"].rearrange("l (c p) -> (l c) p", p=P), 16)
            rows_in("g_ffn", a["g_ffn"].rearrange("l (c p) -> (l c) p", p=P), 16)
            rows_in("g_final", a["g_final"].rearrange("(c p) -> c p", p=P), 8)
            rows_in("conv_k", a["conv_k"].rearrange("l w (c p) -> (l w c) p", p=P), 24)
            rows_in("rwkv_mix", a["rwkv_mix"].rearrange("l w (c p) -> (l w c) p", p=P), 48)
            for name in ("rwkv_w0", "rwkv_a0", "rwkv_k_k", "rwkv_k_a", "rwkv_lnw", "rwkv_lnb"):
                rows_in(name, a[name].rearrange("l (c p) -> (l c) p", p=P), 8)
            rows_in("rwkv_r_k", a["rwkv_r_k"].rearrange("l (c h) n -> (l c) (h n)", h=2), 8)
            rows_in("b_ada0", a["b_ada"][0].rearrange("(c p) -> c p", p=P), 48)
            rows_in("b_ada1", a["b_ada"][1].rearrange("(c p) -> c p", p=P), 48)
            def raw(c):
                for hp in range(2):
                    sp.dma_start(RAW[HS * hp:HS * (hp + 1), c % 2, :, HS * hp:HS * (hp + 1)],
                                 a["state_wkv"][0, :, 2 * c + hp].rearrange("b i j -> i b j")).then_inc(s_raw[c % 2], 16)

            for t, (parts, _) in enumerate(tiles):
                if t >= WRING:
                    sp.wait_ge(bank_ready, tiles[t - WRING][1] + 1)
                if t == WT["wo"]:
                    sp.wait_ge(s_raw0, 1)
                    for c in range(2):
                        raw(c)
                    sp.wait_ge(bank_ready, GROUP["sq2"])
                    sp.wait_ge(bank_free[(GROUP["sq2"] - 1) % BANKS], (GROUP["sq2"] - 1) // BANKS + 1)
                if t == WT["wr"]:
                    sp.wait_ge(s_sel, UNITS * NSEL)
                if t == WT["q1"]:
                    for c in range(2, DC):
                        sp.wait_ge(bank_ready, GROUP["sq2"] + SQ2.index(("turn1", c - 2)) + 1)
                        raw(c)
                    sp.wait_ge(bank_ready, GROUP["gn2"])
                    sp.wait_ge(bank_free[(GROUP["gn2"] - 1) % BANKS], (GROUP["gn2"] - 1) // BANKS + 1)
                if t > 0:
                    load_tile(t)
            sp.wait_ge(s_out, 16 * 3)

        @block.tensor
        def _(pe):
            state = {"n": 0}

            def group(stage, j):
                n = state["n"]
                assert n == GROUP[stage] + j, (stage, j, n)
                state["n"] += 1
                if n >= BANKS:
                    pe.wait_ge(bank_free[n % BANKS], n // BANKS)
                return ps[:, n % BANKS, :]

            def done(ins):
                ins.then_inc(bank_ready, 1)

            def load_wait(t):
                pe.wait_ge(w_load[t % WRING], load_val[t])

            pe.wait_ge(s_const, 1)
            pe.wait_ge(s_cr, 16 * 4)
            o = group("crow", 0)
            for c in range(DC):
                m = pe.transpose(o[:, c * CR_N:(c + 1) * CR_N], CRAW[0:CR_N, c * P:(c + 1) * P], ident[0:CR_N, 0:CR_N])
            done(m)
            pe.wait_ge(s_x, 16 * 3)
            for c in range(DC):
                o = group("x", c)
                for i in range(2):
                    pe.transpose(o[:, i * P:(i + 1) * P], XR[:, i, c * P:(c + 1) * P], ident[:])
                m = pe.transpose(o[:, NP_TOK:TOK], XR[0:NS_TOK, 2, c * P:(c + 1) * P], ident[0:NS_TOK, 0:NS_TOK])
                done(m)
            pe.wait_ge(s_par, 16 * 14)
            o = group("par", 0)
            for i, n in enumerate(PAR_ROWS):
                m = pe.transpose(o[:, i * P:i * P + n], PR[0:n, i, :], ident[0:n, 0:n])
            done(m)

            def ada(stage):
                n = len(ADA_PARTS[stage])

                def turn(j):
                    o = group(stage, ada_cols(j, n))
                    nr = GROUP[stage] + ada_rows(j)
                    pe.wait_ge(bank_free[nr % BANKS], nr // BANKS + 1)
                    for m4 in range(4):
                        m = pe.transpose(o[:, m4 * NCOND:(m4 + 1) * NCOND], ADR[j % 2][0:NCOND, m4 * P:(m4 + 1) * P],
                                         ident[0:NCOND, 0:NCOND])
                    done(m)

                for j in range(n):
                    t = WT[stage] + j
                    load_wait(t)
                    o = group(stage, ada_rows(j))
                    for k in range(DC):
                        m = pe.matmul(o[0:NCOND, :], CT[:, k, 0:NCOND], W[:, t % WRING, k, :], start=(k == 0), stop=(k == DC - 1))
                    done(m)
                    if j > 0:
                        turn(j - 1)
                turn(n - 1)

            pe.wait_ge(s_silu, 2)
            ada("ad0")

            def norm(i):
                o = group(f"nrm{i}", 0)
                for c in range(DC):
                    pe.wait_ge(s_sq, DC * i + c + 1)
                    m = pe.matmul(o[:, 0:TOK], ones[:], SQ[:, c, :], start=(c == 0), stop=(c == DC - 1))
                done(m)

            def turn_keys(layer):
                pe.wait_ge(s_keys, 16 * 2 * (layer + 1))
                for i in range(4):
                    o = group(f"kt{layer}", i)
                    for j in range(4):
                        m = pe.transpose(o[:, j * P:(j + 1) * P], KR[layer][:, i // 2, 4 * (i % 2) + j, :], ident[:])
                    done(m)

            def project(stage, wt, n_out, rhs, first=0, norm_of=None, mixed=False):
                for m0 in range(first, first + n_out):
                    t = WT[wt] + m0 // 4
                    if m0 % 4 == 0:
                        load_wait(t)
                    o = group(stage, m0 - first)
                    for k in range(DC):
                        if norm_of is not None and m0 == first:
                            normed(norm_of, k)
                        if mixed and m0 == first:
                            pe.wait_ge(s_x0, k + 1)
                        m = pe.matmul(o[:, 0:TOK], W[:, t % WRING, k, (m0 % 4) * P:(m0 % 4 + 1) * P], rhs[:, k, :],
                                      start=(k == 0), stop=(k == DC - 1))
                    done(m)

            def normed(i, c=DC - 1):
                pe.wait_ge(s_h, i + 1)
                pe.wait_ge(s_hp, DC * i + c + 1)

            norm(0)
            ada("ad1")
            project("cin", "cin", 24, H, norm_of=0)
            turn_keys(0)
            ada("ad2")
            pe.wait_ge(s_cv, 1)
            project("cout", "cout", DC, CV)
            pe.wait_ge(s_cout, 1)
            for i in range(2):
                o = group("cst", i)
                for c in range(4):
                    m = pe.transpose(o[0:18, c * P:(c + 1) * P], COUT[:, 4 * i + c, :], ident[:])
                done(m)

            def experts(layer):
                norm(2 * layer + 1)
                if layer == 0:
                    ada("ad3")

                def rows_of_h(stage, tile):
                    for i in range(2):
                        o = group(stage, 2 * max(tile - 1, 0) + i)
                        for j in range(4):
                            c = 4 * i + j
                            if tile == 0:
                                normed(2 * layer + 1, c)
                            src = H[:, c, tile * P:(tile + 1) * P] if tile < 2 else HS4[:, c, :]
                            m = pe.transpose(o[:, j * P:(j + 1) * P], src, ident[:])
                        done(m)

                rows_of_h(f"hf{layer}", 0)
                project(f"qa{layer}", f"q{layer}", 4, H)
                pe.wait_ge(s_kt, 4 * (layer + 1))
                pe.wait_ge(s_q, 16 * layer + 4)
                o = group(f"se{layer}", 0)
                for h in range(2):
                    for half in range(2):
                        m = pe.matmul(o[:, (2 * h + half) * P:(2 * h + half + 1) * P], Q[:, 2 * h + half, 0:P], KT[:, half, h, :],
                                      start=True, stop=True)
                done(m)
                project(f"qb{layer}", f"q{layer}", 12, H, 4)
                pe.wait_ge(s_q, 16 * (layer + 1))
                n = 0
                for tile in range(2):
                    for half in range(2):
                        for h4 in range(2):
                            o = group(f"sc{layer}", n)
                            n += 1
                            for j in range(4):
                                h = 4 * h4 + j
                                m = pe.matmul(o[:, j * P:(j + 1) * P], Q[:, 2 * h + half, tile * P:(tile + 1) * P],
                                              KT[:, half, h, :], start=True, stop=True)
                            done(m)
                pe.wait_ge(s_qp, layer + 1)
                o = group(f"sc{layer}", n)
                for half in range(2):
                    for e in range(2):
                        for g in range(4):
                            h = 2 * g + e
                            m = pe.matmul(o[:, (2 * half + e) * P:(2 * half + e + 1) * P], QP[:, 2 * h + half, :],
                                          KT[:, half, h, :], start=(g == 0), stop=(g == 3))
                done(m)
                pe.wait_ge(s_hs4, layer + 1)
                for tile in range(1, 3):
                    rows_of_h(f"ht{layer}", tile)

                if layer == 0:
                    pe.sem_inc(v_free, RING)
                    pe.sem_inc(acc_free, 2)
                u0 = layer * UNITS

                def unit(u, e):
                    pe.wait_ge(acc_free, u + 1)
                    for k in range(TOPK):
                        pe.wait_ge(v_land[k % RING], u * 32 + 16 * (k // RING + 1))
                        pe.wait_ge(s_diag, u * 16 + (k + 1))
                        for i in range(2):
                            m = pe.matmul(ps[:, 4 + 2 * e + i, :], DG[:, k % NDIAG, :],
                                          RVV[:, k % RING, i * 512:(i + 1) * 512], start=(k == 0), stop=(k == TOPK - 1))
                        m.then_inc(v_free, 1)

                with pe.Fori(0, UNITS // 2 - 1) as i:
                    for e in range(2):
                        unit(i * 2 + (u0 + e), e)
                for e in range(2):
                    unit(u0 + UNITS - 2 + e, e)
                pe.wait_ge(s_acc, layer + 1)
                for c in range(DC):
                    o = group(f"res{layer}", c)
                    for i in range(2):
                        pe.matmul(o[:, i * P:(i + 1) * P], OACC[:, i, c * P:(c + 1) * P], ident[:], start=True, stop=True)
                    m = pe.matmul(o[:, NP_TOK:TOK], OACC[:, 2, c * P:(c + 1) * P], sel[:], start=True, stop=True)
                    done(m)

            def evac(stage, j):
                n = GROUP[stage] + j
                pe.wait_ge(bank_free[n % BANKS], n // BANKS + 1)

            def rwkv():
                pe.wait_ge(s_const, 2)
                for i, (stage, wt) in enumerate((("rp", "wr"), ("kp", "wk"), ("vp", "wv"))):
                    if i > 0:
                        pe.wait_ge(s_xi, i + 1)
                    project(stage, wt, DC, (XI0, XI1)[i % 2], mixed=(i == 0))
                    if i == 0:
                        pe.wait_ge(s_sh, 1)
                        for j in range(2):
                            o = group("sst", j)
                            for c in range(4):
                                m = pe.transpose(o[0:NCOND, c * P:(c + 1) * P], COUT[:, 4 * j + c, 0:NCOND], ident[:])
                            done(m)
                load_wait(WT["l1"])
                at0 = 0
                for i, n in enumerate((LW_, LA_, LG_)):
                    pe.wait_ge(s_xi, 4 + i)
                    o = group("lm", i)
                    for k in range(DC):
                        m = pe.matmul(o[0:n, 0:TOK], L1[:, k, at0:at0 + n], (XI1, XI0)[i % 2][:, k, :],
                                      start=(k == 0), stop=(k == DC - 1))
                    done(m)
                    at0 += n
                load_wait(WT["l2"])
                for i, n in enumerate((LW_, LA_, LG_)):
                    evac("lm", i)
                    for c in range(DC):
                        o = group("l2", DC * i + c)
                        done(pe.matmul(o[:, 0:TOK], L2[0:n, i, c * P:(c + 1) * P], LM[0:n, i, :], start=True, stop=True))
                ada("ad5")
                pe.wait_ge(s_kksq, 1)
                for c in range(DC):
                    o = group("kn", c)
                    done(pe.matmul(o[:, 0:TOK], BLK, XI1[:, c, :], start=True, stop=True))
                ada("ad6")
                pe.wait_ge(s_rk, 1)
                for c in range(DC):
                    o = group("bn", c)
                    done(pe.matmul(o[:, 0:TOK], BLK, XI1[:, c, :], start=True, stop=True))
                ada("ad7")
                def turn_y(tile):
                    n = P if tile < 2 else NS_TOK
                    pe.wait_ge(s_yn, tile + 1)
                    for q in range(2):
                        o = group(f"gn{tile}", q)
                        for j in range(4):
                            m = pe.transpose(o[:, j * n:(j + 1) * n], YR[0:n, (4 * q + j) * P:(4 * q + j + 1) * P], ident[0:n, 0:n])
                        done(m)

                pe.wait_ge(s_wkv, 1)
                for tile in range(3):
                    n = P if tile < 2 else NS_TOK
                    t0 = tile * P
                    for i in range(3):
                        for q in range(2):
                            o = group(f"tm{tile}", 2 * i + q)
                            for j in range(4):
                                c = 4 * q + j
                                src = (VF, BF, KF)[i][:, c, t0:t0 + n] if tile < 2 or i == 0 else BBS[:, i - 1, c, :]
                                m = pe.transpose(o[0:n, j * P:(j + 1) * P], src, ident[:])
                            done(m)
                    nm = f"nm{tile}"
                    steps = NM_STEPS if tile < 2 else NM_STEPS_S

                    def head(f, h):
                        return f[HS * (h % 2):HS * (h % 2) + HS, h // 2, t0:t0 + n]

                    for bp in range(2):
                        for step in range(steps):
                            for b in range(2):
                                def need(*which):
                                    for w in which:
                                        evac(nm + "ab"[bp], w * 2 + b)

                                o = group(nm + "ab"[bp], step * 2 + b)
                                T = NT[0:n, b, :, :, 0:n]
                                heads = [2 * (4 * bp + j) + b for j in range(4)]
                                G = (GG[0:n, 3] if tile < 2 else GS[3][0:n])[:, slot(heads[0]):slot(heads[0]) + 4, :]
                                A8, U8, A2, U2, TT = (T[:, i] for i in range(5))
                                if step < 5:
                                    ops = [(BF, AF), (AF, BF), (KF, AF), (BF, RF), (KF, RF)][step]
                                    for j, h in enumerate(heads):
                                        m = pe.matmul(o[0:n, j * n:(j + 1) * n], head(ops[0], h), head(ops[1], h),
                                                      start=True, stop=True)
                                    done(m)
                                    continue
                                if tile == 2:
                                    if step == 5:
                                        need(0, 1)
                                    else:
                                        need(5)
                                    l, r = {5: (U8, A8), 6: (A2, G)}[step]
                                else:
                                    need(*{5: (0, 1), 7: (6,), 8: (5,), 11: (10, 7), 12: (9, 8), 13: (11,), 14: (12, 13),
                                           16: (14,), 17: (15, 16), 19: (17,), 20: (18, 19)}.get(step, ()))
                                    l, r = {5: (A8, U8), 6: (U8, A8), 7: (A2, G), 8: (U2, TT), 9: (A2, U2), 10: (U2, A2),
                                            11: (A8, G), 12: (U8, TT), 13: (T[:, 5], G), 14: (TT, A2), 15: (A2, TT),
                                            16: (T[:, 6], G), 17: (TT, A2), 18: (A2, TT), 19: (T[:, 7], G),
                                            20: (TT, A2)}[step]
                                for j in range(4):
                                    m = pe.matmul(o[0:n, j * n:(j + 1) * n], l[:, j, :], r[:, j, :], start=True, stop=True)
                                done(m)
                        if tile > 0 and bp == 0:
                            turn_y(tile - 1)

                    def made(*which):
                        for bp in range(2):
                            for b in range(2):
                                for w in which:
                                    evac(nm + "ab"[bp], w * 2 + b)

                    for j in range(6):
                        evac(f"tm{tile}", j)
                    made(2, 4)
                    if tile < 2:
                        sq = f"sq{tile}"
                        for ch in range(2):
                            rows = slice(HS * ch, HS * ch + HS)
                            if ch == 0 and tile == 0:
                                pe.wait_ge(s_wkv, 2)
                            elif ch == 0:
                                evac("sq0", 12)
                                evac("sq0", 13)
                            else:
                                evac(sq, 4)
                                evac(sq, 5)
                            for q in range(2):
                                o = group(sq, 8 * ch + q)
                                for j in range(4):
                                    c = 4 * q + j
                                    pe.matmul(o[:, j * P:(j + 1) * P], AF[:, c, t0:t0 + P], state_of(2 * tile + ch, c), start=True, stop=False,
                                              skip_group_check=True)
                                    for hp in range(2):
                                        h = 2 * c + hp
                                        m = pe.matmul(o[:, h % 8 * HS:h % 8 * HS + HS], GG[:, 0, slot(h), :], VT[:, h * HS:(h + 1) * HS],
                                                      start=False, stop=True, skip_group_check=True)
                                done(m)
                            if ch == 0:
                                made(steps - 1, 3)
                            for q in range(2):
                                evac(sq, 8 * ch + q)
                                o = group(sq, 8 * ch + 2 + q)
                                for j in range(8):
                                    h = 8 * q + j
                                    m = pe.matmul(o[:, j * HS:(j + 1) * HS], GG[:, 3, slot(h), :], RH[:, h // 2, HS * (h % 2):HS * (h % 2) + HS],
                                                  start=True, stop=True)
                                done(m)
                            for q in range(2):
                                evac(sq, 8 * ch + 2 + q)
                                o = group(sq, 8 * ch + 4 + q)
                                for j in range(4):
                                    c = 4 * q + j
                                    oc = o[:, j * P:(j + 1) * P]
                                    pe.matmul(oc, ident[:], state_of(2 * tile + ch, c), start=True, stop=False)
                                    pe.matmul(oc, BT[rows, c * P:(c + 1) * P], SA[rows, c, :], start=False, stop=False)
                                    m = pe.matmul(oc, KTK[rows, c * P:(c + 1) * P], VT[rows, c * P:(c + 1) * P], start=False, stop=True)
                                done(m)
                            for q in range(2):
                                o = group(sq, 8 * ch + 6 + q)
                                for j in range(4):
                                    c = 4 * q + j
                                    pe.matmul(o[:, j * P:(j + 1) * P], RF[:, c, t0:t0 + P], state_of(2 * tile + ch, c), start=True, stop=False,
                                              skip_group_check=True)
                                    for hp in range(2):
                                        h = 2 * c + hp
                                        oh = o[:, h % 8 * HS:h % 8 * HS + HS]
                                        pe.matmul(oh, GG[:, 1, slot(h), :], SA[:, c, HS * hp:HS * hp + HS], start=False, stop=False,
                                                  skip_group_check=True)
                                        m = pe.matmul(oh, GG[:, 2, slot(h), :], VT[:, h * HS:(h + 1) * HS], start=False, stop=True,
                                                      skip_group_check=True)
                                done(m)
                        if tile == 1:
                            evac(sq, 12)
                            evac(sq, 13)
                            for q in range(2):
                                o = group("pso", q)
                                for j in range(4):
                                    m = pe.transpose(o[:, j * P:(j + 1) * P], SB[:, 4 * q + j, :], ident[:])
                                done(m)
                    else:
                        def sample_step(kind, c):
                            o = group("sq2", SQ2.index((kind, c)))
                            def pair(o, lhsT, rhs, start):
                                for hp in range(2):
                                    m = pe.matmul(o[:, HS * hp:HS * hp + HS], lhsT(slot(2 * c + hp)), rhs[:, HS * hp:HS * hp + HS],
                                                  start=start, stop=True, skip_group_check=True)
                                return m

                            if kind in ("turn0", "turn1"):
                                half = int(kind[-1])
                                if half == 0:
                                    pe.wait_ge(s_raw[c % 2], 32 * (c // 2 + 1))
                                for j in range(4):
                                    m = pe.transpose(o[:, j * P:(j + 1) * P], RAW[:, c % 2, 4 * half + j, :], ident[:])
                            elif kind == "right":
                                pe.wait_ge(s_atm, c + 1)
                                evac("sq2", SQ2.index(("turn0", c)))
                                evac("sq2", SQ2.index(("turn1", c)))
                                o = o[0:2 * n, 0:P]
                                for q in range(NSEQ):
                                    pe.matmul(o, ART[:, c % 2, q].rearrange("p r t -> p (r t)"), SS[:, c % 2, q, :],
                                              start=(q == 0), stop=False, skip_group_check=True)
                                m = pair(o, lambda h: GKV[0:n, h].rearrange("p r t -> p (r t)"), VT[0:n, c * P:(c + 1) * P], False)
                            elif kind == "sa":
                                if c == 0:
                                    made(steps - 1, 3)
                                evac("sq2", SQ2.index(("right", c)))
                                m = pair(o[0:n], lambda h: GS[3][0:n, h, :], RHS[0:n], True)
                            elif kind == "y":
                                evac("sq2", SQ2.index(("sa", c)))
                                m = pair(o[0:n], lambda h: GS[1][0:n, h, :], SAV[0:n, c * P:(c + 1) * P], True)
                            elif kind in ("new0", "new1"):
                                half = int(kind[-1])
                                pe.wait_ge(s_sam, c + 1)
                                m = pe.matmul(o, BT[0:2 * n, c * P:(c + 1) * P],
                                              SAVM[0:2 * n, 4 * half:4 * half + 4, :].rearrange("p s n -> p (s n)"), start=True, stop=True)
                            else:
                                half = int(kind[-1])
                                evac("sq2", SQ2.index((f"new{half}", c)))
                                for j in range(4):
                                    m = pe.transpose(o[:, j * P:(j + 1) * P], NEW[:, c % 2, 4 * half + j, :], ident[:])
                            done(m)

                        for kind, c in SQ2:
                            sample_step(kind, c)
                turn_y(2)
                pe.wait_ge(s_wy, 1)
                project("wo", "wo", DC, H)

            experts(0)
            norm(2)
            ada("ad4")
            rwkv()
            turn_keys(1)
            experts(1)
            norm(4)
            for tile in range(3):
                n = P if tile < 2 else NS_TOK
                for i in range(2):
                    o = group("fin", 2 * tile + i)
                    for j in range(4):
                        if tile == 0:
                            pe.wait_ge(s_hf, 4 * i + j + 1)
                        m = pe.transpose(o[0:n, j * P:(j + 1) * P], H[:, 4 * i + j, tile * P:tile * P + n], ident[:])
                    done(m)

        @block.scalar
        def _(act):
            act.dma_start(CRAW[CR_COND:CR_COND + 1, :], a["c_prompt"]).then_inc(s_cr, 16)
            act.dma_start(CRAW[CR_COND + 1:CR_COND + NCOND, :], a["c_sample"]).then_inc(s_cr, 16)
            act.dma_start(CRAW[CR_CONV:CR_CONV + 16, :], a["state_conv"].rearrange("l b w d -> (l b w) d")).then_inc(s_cr, 16)
            act.dma_start(CRAW[CR_SHIFT:CR_SHIFT + 8, :], a["state_shift"].rearrange("l b d -> (l b) d")).then_inc(s_cr, 16)
            for i in range(2):
                act.dma_start(XR[:, i, :], a["x_prompt"][0, i * P:(i + 1) * P, :]).then_inc(s_x, 16)
            act.dma_start(XR[0:NS_TOK, 2, :], a["x_sample"].rearrange("b t d -> (b t) d")).then_inc(s_x, 16)

            def load_keys(layer):
                for half, k in enumerate(("peer_k1", "peer_k2")):
                    act.dma_start(KR[layer][:, half, :, :], a[k][layer].rearrange("h k d -> k h d")).then_inc(s_keys, 16)

            load_keys(0)

            def take(stage, j):
                n = GROUP[stage] + j
                act.wait_ge(bank_ready, n + 1)
                return ps[:, n % BANKS, :], bank_free[n % BANKS]

            o, free = take("crow", 0)
            ov = o[:, 0:DC * CR_N].rearrange("p (c n) -> p c n", c=DC)
            act.activation(CT[:, :, 0:NCOND], ov[:, :, 0:NCOND], ACT.Silu).then_inc(s_silu, 1)
            act.activation(CT[:, :, NCOND:CR_N], ov[:, :, NCOND:CR_N], ACT.Copy).then_inc(s_silu, 1)
            act.wait_ge(s_silu, 2)
            act.sem_inc(free, 1)

            def copy(stage, j, dst, src=lambda o: o, func=ACT.Copy, **kw):
                o, free = take(stage, j)
                act.activation(dst, src(o), func, **kw).then_inc(free, 1)

            def taken(stage, j):
                n = GROUP[stage] + j
                act.wait_ge(bank_free[n % BANKS], n // BANKS + 1)

            def ada(stage, between={}):
                n = len(ADA_PARTS[stage])

                def columns(j):
                    o, free = take(stage, ada_cols(j, n))
                    for m4 in range(4):
                        layer, m0 = ADA_PARTS[stage][j][0], 4 * ADA_PARTS[stage][j][1]
                        m = act.activation(ADA[:, layer, m0 + m4, :], o[:, m4 * NCOND:(m4 + 1) * NCOND], ACT.Identity,
                                           bias=col(f"b_ada{layer}", m0 + m4))
                    m.then_inc(free, 1)

                for j in range(n):
                    copy(stage, ada_rows(j), ADR[j % 2][0:NCOND, :], lambda o: o[0:NCOND, :])
                    if j > 0:
                        columns(j - 1)
                    if j in between:
                        between[j]()
                columns(n - 1)

            taken("par", 0)

            def squares(i):
                for c in range(DC):
                    act.wait_ge(s_xready, DC * i + c + 1)
                    act.activation(SQ[:, c, :], X[:, c, :], ACT.Square).then_inc(s_sq, 1)

            squares(0)
            ada("ad0")

            def keys(layer):
                for i in range(4):
                    o, free = take(f"kt{layer}", i)
                    act.activation(KT[:, i // 2, 4 * (i % 2):4 * (i % 2) + 4, :],
                                   o.rearrange("p (h k) -> p h k", h=4), ACT.Copy).then_inc(s_kt, 1)
                    act.wait_ge(s_kt, 4 * layer + i + 1)
                    act.sem_inc(free, 1)

            def root_and_h(i):
                if i == 3:
                    keys(1)
                act.wait_ge(s_ms, i + 1)
                act.activation(rms[:], rms[:], ACT.Sqrt).then_inc(s_rms, 1)
                if i < 4:
                    for c in range(DC):
                        act.wait_ge(s_hn, DC * i + c + 1)
                        act.activation(H[:, c, 0:NP_TOK], HN[:, c, 0:NP_TOK], ACT.Identity, scale=GA[:, i, c, 0:1],
                                       bias=shift_of(i)[:, c, 0:1]).then_inc(s_hp, 1)

            root_and_h(0)
            ada("ad1")
            for m in range(16):
                o, free = take("cin", m)
                dst = (BG if m < 8 else CG)[:, m % 8, :]
                act.activation(dst, o[:, 0:TOK], ACT.Copy).then_inc(free, 1)
                if m == 15:
                    act.wait_ge(free, (GROUP["cin"] + m) // BANKS + 1)
                    act.sem_inc(s_gates, 1)
            keys(0)
            ada("ad2")
            for i in range(2):
                o, free = take("cst", i)
                if i == 0:
                    act.wait_ge(s_cv, 1)
                act.activation(CROW[0:18, i * 512:(i + 1) * 512], o[0:18, :], ACT.Copy).then_inc(free, 1)
                act.wait_ge(free, (GROUP["cst"] + i) // BANKS + 1)
            act.dma_start(out[2].rearrange("l b w d -> (l b w) d"), CROW[0:2, :]).then_inc(s_crow, 16)
            act.dma_start(out[5].rearrange("l b w d -> (l b w) d"), CROW[2:18, :]).then_inc(s_crow, 16)

            def experts(layer):
                squares(2 * layer + 1)
                root_and_h(2 * layer + 1)
                if layer == 0:
                    ada("ad3")
                for i in range(2):
                    copy(f"hf{layer}", i, HTOK[:, 0, i * 512:(i + 1) * 512])

                def query(m):
                    o, free = take(f"qa{layer}", m) if m < 4 else take(f"qb{layer}", m - 4)
                    act.activation(Q[:, m, :], o[:, 0:TOK], ACT.Copy).then_inc(s_q, 1)
                    act.wait_ge(s_q, 16 * layer + m + 1)
                    act.sem_inc(free, 1)

                u0 = layer * UNITS

                def gate_exp(u, e):
                    act.wait_ge(s_sel, u * NSEL + SEL_IDX)
                    act.activation(GATE[:, e, :], GATE[:, e, :], ACT.Exp).then_inc(s_gexp, 1)

                for m in range(4):
                    query(m)
                o, free = take(f"se{layer}", 0)
                for e in range(2):
                    act.activation(SCUR[:, e].rearrange("p a k -> p (a k)"), o[:, 2 * e * P:2 * (e + 1) * P], ACT.Copy).then_inc(s_scur, 1)
                act.wait_ge(s_scur, u0 + 2)
                act.sem_inc(free, 1)
                for m in range(4, 16):
                    query(m)
                    if m == GEXP_AT[0]:
                        gate_exp(u0, 0)
                    if m == GEXP_AT[1]:
                        gate_exp(u0 + 1, 1)
                for n in range(8):
                    tile, half, h4 = n // 4, (n // 2) % 2, n % 2
                    copy(f"sc{layer}", n, SCALL[:, 8 * tile + 4 * h4:8 * tile + 4 * h4 + 4, half * NKEYS:(half + 1) * NKEYS],
                         lambda o: o.rearrange("p (h k) -> p h k", h=4))
                copy(f"sc{layer}", 8, SCALL[:, 16:18, :].rearrange("p e (a k) -> p a e k", a=2),
                     lambda o: o.rearrange("p (a e k) -> p a e k", a=2, e=2))
                for tile in range(1, 3):
                    for i in range(2):
                        copy(f"ht{layer}", 2 * tile - 2 + i, HTOK[:, tile, i * 512:(i + 1) * 512])
                for j in range(9):
                    taken(f"sc{layer}", j)

                def unit(u, lu, e, last):
                    if not last:
                        act.wait_ge(s_sel, u * NSEL + NSEL)
                        act.sem_inc(s_actgo, 1)
                        act.activation(SCUR[:, e].rearrange("p a k -> p (a k)"), at(SCALL, lu + 2), ACT.Copy).then_inc(s_scur, 1)
                    act.wait_ge(s_z, u * 16 + 16)
                    act.activation(GL[:, e, :], ZB[:, e, :], ACT.Gelu).then_inc(s_gelu, 1)
                    act.wait_ge(s_coef, u + 1)
                    for k in range(TOPK):
                        if k == 14 and not last:
                            gate_exp(u + 2, e)
                        act.wait_ge(v_free, u * 16 + (k + RING - NDIAG + 1))
                        act.activation(DG[:, k % NDIAG, :], ident[:], ACT.Copy, scale=CF[:, e, k:k + 1]).then_inc(s_diag, 1)

                with act.Fori(0, UNITS // 2 - 1) as i:
                    for e in range(2):
                        unit(i * 2 + (u0 + e), i * 2 + e, e, False)
                for e in range(2):
                    unit(u0 + UNITS - 2 + e, UNITS - 2 + e, e, True)

            def rwkv():
                for stage, dst in (("rp", RF), ("kp", KF), ("vp", VF)):
                    for c in range(DC):
                        copy(stage, c, dst[:, c, :], lambda o: o[:, 0:TOK])
                    if stage == "rp":
                        for i in range(2):
                            copy("sst", i, CROW2[0:NCOND, i * 512:(i + 1) * 512], lambda o: o[0:NCOND, :])
                            taken("sst", i)
                        act.dma_start(out[3][0], CROW2[0:1, :]).then_inc(s_shr, 16)
                        act.dma_start(out[6][0], CROW2[1:NCOND, :]).then_inc(s_shr, 16)
                copy("lm", 0, LM[0:LW_, 0, :], lambda o: o[0:LW_, 0:TOK], ACT.Tanh)
                copy("lm", 1, LM[0:LA_, 1, :], lambda o: o[0:LA_, 0:TOK])
                copy("lm", 2, LM[0:LG_, 2, :], lambda o: o[0:LG_, 0:TOK], ACT.Sigmoid)
                for c in range(DC):
                    copy("l2", c, LW[:, c, :], lambda o: o[:, 0:TOK], ACT.Sigmoid, bias=col("rwkv_w0", c))
                for c in range(DC):
                    copy("l2", DC + c, BF[:, c, :], lambda o: o[:, 0:TOK], ACT.Sigmoid, bias=col("rwkv_a0", c))
                for c in range(DC):
                    copy("l2", 2 * DC + c, GF[:, c, :], lambda o: o[:, 0:TOK])
                for j in range(3):
                    taken("l2", 20 + j)
                taken("l2", 23)
                act.sem_inc(s_sg, 1)
                act.wait_ge(s_kk, 1)
                act.activation(XI1, AF, ACT.Square).then_inc(s_kksq, 1)
                ada("ad5")
                act.wait_ge(s_kkn, 1)
                act.activation(XI0, XI0, ACT.Sqrt).then_inc(s_kkr, 1)
                ada("ad6")
                def exps():
                    act.wait_ge(s_dc, 1)
                    act.activation(XI1, XI0, ACT.Exp).then_inc(s_ex, 1)
                    act.activation(FE[:], FE[:], ACT.Exp).then_inc(s_ex, 1)
                    act.activation(EC[:], EC[:], ACT.Exp).then_inc(s_ex, 1)

                def exps_minus():
                    act.wait_ge(s_exu, 1)
                    act.activation(XI1, XI0, ACT.Exp, scale=-1.0).then_inc(s_ex, 1)
                    act.wait_ge(s_exu, 2)
                    act.activation(LW, LW, ACT.Exp).then_inc(s_ex, 1)

                ada("ad7", {0: exps, 1: exps_minus})
                def gn_root(tile):
                    n = P if tile < 2 else NS_TOK
                    act.wait_ge(s_gn, tile + 1)
                    act.activation(gst[0:n, 1, :], gst[0:n, 1, :], ACT.Sqrt).then_inc(s_gnr, 1)

                for tile in range(3):
                    n = P if tile < 2 else NS_TOK
                    for i in range(3):
                        for q in range(2):
                            dst = (VT, BT, KTK)[i][0:n] if tile < 2 or i < 2 else BT[n:2 * n]
                            copy(f"tm{tile}", 2 * i + q, dst[:, q * 512:(q + 1) * 512], lambda o: o[0:n, :])
                            if tile == 2 and i == 1 and q == 0:
                                for j in range(2):
                                    taken("tm2", j)
                                act.activation(SAV[n:2 * n, :], VT[0:n, :], ACT.Copy).then_inc(s_v2, 1)
                    steps = NM_STEPS if tile < 2 else NM_STEPS_S
                    to = {5: 3, 6: 2, 9: 1, 10: 0, 13: 2, 16: 2, 19: 2} if tile < 2 else {5: 2}
                    for bp in range(2):
                        for step in sorted(to):
                            for b in range(2):
                                copy(f"nm{tile}" + "ab"[bp], step * 2 + b, NT[0:n, b, to[step], :, 0:n],
                                     lambda o: o[0:n, 0:4 * n].rearrange("p (h t) -> p h t", h=4))
                            if tile > 0 and bp == 0 and b == 1 and step == (6 if tile == 1 else 5):
                                gn_root(tile - 1)
                    if tile < 2:
                        for ch in range(2):
                            rows = slice(HS * ch, HS * ch + HS)
                            for q in range(2):
                                copy(f"sq{tile}", 8 * ch + q, RH[:, 4 * q:4 * q + 4, :], lambda o: o.rearrange("p (c i) -> p c i", c=4))
                            for q in range(2):
                                copy(f"sq{tile}", 8 * ch + 2 + q, SA[:, 4 * q:4 * q + 4, :], lambda o: o.rearrange("p (c i) -> p c i", c=4))
                            for q in range(2):
                                copy(f"sq{tile}", 8 * ch + 6 + q, YR[rows, q * 512:(q + 1) * 512], lambda o: o[rows, :])
                        if tile == 1:
                            for q in range(2):
                                copy("pso", q, PSO[:, 4 * q:4 * q + 4, :], lambda o: o.rearrange("p (c j) -> p c j", c=4))
                                taken("pso", q)
                            for hp in range(2):
                                act.dma_start(out[4][0, 0].rearrange("(c h) i j -> h i c j", h=2)[hp],
                                              PSO[HS * hp:HS * hp + HS, :, HS * hp:HS * hp + HS]).then_inc(s_shr, 16)
                    else:
                        act.wait_ge(s_shr, 64)
                        for kind, c in SQ2:
                            half = int(kind[-1]) if kind[-1].isdigit() else 0
                            four = lambda o: o.rearrange("p (s n) -> p s n", s=4)
                            if kind in ("turn0", "turn1"):
                                if half == 0 and c >= 2:
                                    act.wait_ge(s_kept, c - 1)
                                copy("sq2", SQ2.index((kind, c)), SS[:, c % 2, 4 * half:4 * half + 4, :], four)
                            elif kind in ("out0", "out1"):
                                if half == 0 and c >= 2:
                                    act.wait_ge(s_stout[c % 2], 32 * (c // 2))
                                copy("sq2", SQ2.index((kind, c)), OUTB[:, c % 2, 4 * half:4 * half + 4, :], four)
                                if half == 1:
                                    for k in ("out0", "out1"):
                                        taken("sq2", SQ2.index((k, c)))
                                    for hp in range(2):
                                        act.dma_start(out[7][0, :, 2 * c + hp].rearrange("b i j -> i b j"),
                                                      OUTB[HS * hp:HS * hp + HS, c % 2, :, HS * hp:HS * hp + HS]).then_inc(s_stout[c % 2], 16)
                gn_root(2)
                act.wait_ge(s_yn, 3)
                load_keys(1)
                for i in range(2):
                    act.wait_ge(s_stout[i], 16 * DC)

            experts(0)
            squares(2)
            root_and_h(2)
            ada("ad4")
            rwkv()
            experts(1)
            squares(4)
            root_and_h(4)
            for tile in range(3):
                n = P if tile < 2 else NS_TOK
                for i in range(2):
                    o, free = take("fin", 2 * tile + i)
                    act.activation(YT[0:n, tile, i * 512:(i + 1) * 512], o[0:n, :], ACT.Copy).then_inc(s_yt, 1)
                    act.wait_ge(s_yt, 2 * tile + i + 1)
                    act.sem_inc(free, 1)
                dst = out[0][0, tile * P:(tile + 1) * P, :] if tile < 2 else out[1].rearrange("b t d -> (b t) d")
                act.dma_start(dst, YT[0:n, tile, :]).then_inc(s_out, 16)

        @block.vector
        def _(v):
            V = Steps(v, dve_step)

            def take(stage, j):
                n = GROUP[stage] + j
                v.wait_ge(bank_ready, n + 1)
                return ps[:, n % BANKS, :], bank_free[n % BANKS]

            def free_bank(free):
                V.sync()
                v.sem_inc(free, 1)

            v.wait_ge(s_const, 1)
            V.chain(v.tensor_tensor(sel[:], ident[:, 0:32], ident[:, 32:64], ALU.add))
            V.chain(v.tensor_tensor(sel[:], sel[:], ident[:, 64:96], ALU.add))
            V.chain(v.tensor_tensor(sel[:], sel[:], ident[:, 96:128], ALU.add))
            for c in range(DC):
                o, free = take("x", c)
                V.do(v.tensor_copy(X[:, c, :], o[:, 0:TOK]))
                free_bank(free)
                v.sem_inc(s_xready, 1)
            o, free = take("par", 0)
            for i, n in enumerate(PAR_ROWS):
                V.do(v.tensor_copy(PAR[:, i * P:i * P + n], o[:, i * P:i * P + n]))
            free_bank(free)

            def gains(stage, which):
                last = GROUP[stage] + 2 * len(ADA_PARTS[stage]) - 1
                v.wait_ge(bank_free[last % BANKS], last // BANKS + 1)
                for w in which:
                    g = cols("g_mix", 16) if w % 2 == 0 else cols("g_ffn", 16)
                    g = g[:, 8 * (w // 2):8 * (w // 2) + 8].unsqueeze(2).broadcast_to([P, DC, NCOND])
                    V.do(v.scalar_tensor_tensor(GA[:, w], scale_of(w), 1.0, g, ALU.add, ALU.mult))
                V.sync()

            gains("ad0", (0,))

            def norm(i):
                o, free = take(f"nrm{i}", 0)
                V.do(v.tensor_scalar(rms[:], o[:, 0:TOK], 1.0 / D, EPS, ALU.mult, ALU.add), s_ms)
                free_bank(free)
                v.wait_ge(s_rms, i + 1)
                V.chain(v.reciprocal(rstd[:], rms[:]))
                if i < 4:
                    V.chain(v.tensor_tensor(HN[:, :, NP_TOK:TOK], X[:, :, NP_TOK:TOK],
                                            rstd[:, NP_TOK:TOK].unsqueeze(1).broadcast_to([P, DC, NS_TOK]), ALU.mult))
                    V.do(v.tensor_tensor(HN[:, 0, 0:NP_TOK], X[:, 0, 0:NP_TOK], rstd[:, 0:NP_TOK], ALU.mult), s_hn)
                    V.chain(v.tensor_tensor(sample(HN), sample(HN), per_step(GA[:, i]), ALU.mult))
                    V.chain(v.tensor_tensor(sample(H), sample(HN), per_step(shift_of(i)), ALU.add))
                    v.sem_inc(s_h, 1)
                    for c in range(1, DC):
                        V.do(v.tensor_tensor(HN[:, c, 0:NP_TOK], X[:, c, 0:NP_TOK], rstd[:, 0:NP_TOK], ALU.mult), s_hn)
                    V.sync()
                else:
                    for c in range(DC):
                        V.do(v.scalar_tensor_tensor(H[:, c, :], X[:, c, :], col("g_final", c), rstd[:], ALU.mult, ALU.mult), s_hf)

            def residual(stage, which):
                g = gate_of(which)
                for c in range(DC):
                    o, free = take(stage, c)
                    V.do(v.scalar_tensor_tensor(X[:, c, 0:NP_TOK], o[:, 0:NP_TOK], g[:, c, 0:1], X[:, c, 0:NP_TOK],
                                                ALU.mult, ALU.add))
                    gs = g[:, c, 1:NCOND].unsqueeze(2).broadcast_to([P, NSEQ, NSTEP])
                    tv = tmpS[:, c % 2, :].rearrange("p (b t) -> p b t", b=NSEQ)
                    V.do(v.tensor_tensor(tv, o[:, NP_TOK:TOK].rearrange("p (b t) -> p b t", b=NSEQ), gs, ALU.mult))
                    free_bank(free)
                    V.do(v.tensor_tensor(X[:, c, NP_TOK:TOK], X[:, c, NP_TOK:TOK], tmpS[:, c % 2, :], ALU.add))
                    V.sync()
                    v.sem_inc(s_xready, 1)

            norm(0)
            gains("ad1", (1, 2))
            sampleU = UH[:, :, NP_TOK + 2:].rearrange("p c (b t) -> p c b t", b=NSEQ)
            V.do(v.memset(UH[:, :, 0:2], 0.0))
            V.do(v.tensor_copy(sampleU[:, :, :, 0:2], CT[:, :, CR_CONV:CR_CONV + 16].rearrange("p c (b w) -> p c b w", b=NSEQ)))
            v.wait_ge(s_gates, 1)
            cs = CS.rearrange("p (c b t) -> p c b t", c=DC, b=NSEQ)
            for c in range(DC):
                o, free = take("cin", 16 + c)
                V.do(v.tensor_tensor(UH[:, c, 2:NP_TOK + 2], o[:, 0:NP_TOK], CG[:, c, 0:NP_TOK], ALU.mult))
                V.do(v.tensor_tensor(sampleU[:, c, :, 2:6], o[:, NP_TOK:TOK].rearrange("p (b t) -> p b t", b=NSEQ),
                                     CG[:, c, NP_TOK:TOK].rearrange("p (b t) -> p b t", b=NSEQ), ALU.mult))
                free_bank(free)
                for j in range(3):
                    k = col("conv_k", 8 * j + c)
                    for dst, src in ((CV[:, c, 0:NP_TOK], UH[:, c, j:j + NP_TOK]), (cs[:, c], sampleU[:, c, :, j:j + 4])):
                        if j == 0:
                            V.do(v.tensor_scalar(dst, src, k, None, ALU.mult))
                        else:
                            V.do(v.scalar_tensor_tensor(dst, src, k, dst, ALU.mult, ALU.add))
                    V.sync()
                V.do(v.tensor_tensor(CV[:, c, 0:NP_TOK], CV[:, c, 0:NP_TOK], BG[:, c, 0:NP_TOK], ALU.mult))
                V.do(v.tensor_tensor(sample(CV)[:, c], cs[:, c], sample(BG)[:, c], ALU.mult))
            V.sync()
            v.sem_inc(s_cv, 1)
            V.do(v.tensor_copy(COUT[:, :, 0:2], UH[:, :, NP_TOK:NP_TOK + 2]))
            V.do(v.tensor_copy(COUT[:, :, 2:18].rearrange("p c (b w) -> p c b w", b=NSEQ), sampleU[:, :, :, 4:6]))
            V.sync()
            v.sem_inc(s_cout, 1)
            residual("cout", 0)

            def choose(u, e, layer):
                state = {"j": 0}

                def step(make, back=1):
                    j = state["j"]
                    state["j"] += 1
                    if not isinstance(u, int) or u * NSEL + j + 1 - back > 0:
                        v.wait_ge(s_sel, u * NSEL + (j + 1 - back))
                    v.sem_inc(s_selgo, 1)
                    make().then_inc(s_sel, 1)

                s0, s1 = SCUR[:, e, 0, :], SCUR[:, e, 1, :]
                r0, r1 = REST[:, 0, 0:NKEYS], REST[:, 1, 0:NKEYS]
                grid = [P, TOPK, TOPK]
                square = lambda x: x.rearrange("p (a b) -> p a b", a=TOPK)
                v.wait_ge(s_scur, u + 1)
                v.sem_inc(s_selgo, 1)
                step(lambda: v.max(VAL[:, 0, 0:8], s0))
                step(lambda: v.max(VAL[:, 1, 0:8], s1), 2)
                yield
                step(lambda: v.max_index(KEY[:, 0, 0:8], VAL[:, 0, 0:8], s0), 2)
                step(lambda: v.match_replace(r0, VAL[:, 0, 0:8], s0, NEG), 3)
                yield
                step(lambda: v.max_index(KEY[:, 1, 0:8], VAL[:, 1, 0:8], s1), 3)
                step(lambda: v.match_replace(r1, VAL[:, 1, 0:8], s1, NEG), 4)
                yield
                step(lambda: v.max(VAL[:, 0, 8:16], r0), 3)
                step(lambda: v.max(VAL[:, 1, 8:16], r1), 2)
                yield
                step(lambda: v.max_index(KEY[:, 0, 8:16], VAL[:, 0, 8:16], r0), 2)
                step(lambda: v.max_index(KEY[:, 1, 8:16], VAL[:, 1, 8:16], r1), 2)
                yield
                step(lambda: v.tensor_tensor(square(CAND), VAL[:, 0].unsqueeze(2).broadcast_to(grid),
                                             VAL[:, 1].unsqueeze(1).broadcast_to(grid), ALU.add), 3)
                step(lambda: v.max(BEST[:, 0:8], CAND))
                yield
                step(lambda: v.max_index(AT[:, 0:8], BEST[:, 0:8], CAND))
                step(lambda: v.match_replace(REST[:, 0, :], BEST[:, 0:8], CAND, NEG), 2)
                yield
                step(lambda: v.max(BEST[:, 8:16], REST[:, 0, :]))
                step(lambda: v.max_index(AT[:, 8:16], BEST[:, 8:16], REST[:, 0, :]))
                yield
                step(lambda: v.tensor_scalar(POS[:, 0], AT, 4, None, ALU.logical_shift_right))
                step(lambda: v.tensor_scalar(POS[:, 1], AT, TOPK - 1, None, ALU.bitwise_and), 2)
                io = iota16[:].unsqueeze(1).broadcast_to(grid)
                yield
                step(lambda: v.tensor_tensor(square(ONEHOT[:, 0]), POS[:, 0].unsqueeze(2).broadcast_to(grid), io, ALU.is_equal), 2)
                step(lambda: v.tensor_tensor(square(ONEHOT[:, 1]), POS[:, 1].unsqueeze(2).broadcast_to(grid), io, ALU.is_equal), 2)
                yield
                for i in range(2):
                    step(lambda: v.tensor_tensor(square(ONEHOT[:, i]), square(ONEHOT[:, i]),
                                                 KEY[:, i].unsqueeze(1).broadcast_to(grid), ALU.mult), 2)
                yield
                step(lambda: v.tensor_reduce(KEYF, ONEHOT.rearrange("p i (a b) -> p i a b", a=TOPK), AX_X, ALU.add))
                step(lambda: v.scalar_tensor_tensor(IDX[:, e], KEYF[:, 0], float(NKEYS), KEYF[:, 1], ALU.mult, ALU.add))
                yield
                step(lambda: v.tensor_scalar(CURU[:, e, :], IDX[:, e], float(layer * NEXP), None, ALU.add))
                step(lambda: v.tensor_tensor(GATE[:, e], BEST, BEST[:, 0:1].broadcast_to([P, TOPK]), ALU.subtract), 2)
                assert state["j"] == SEL_IDX
                yield
                v.wait_ge(s_gexp, u + 1)
                v.sem_inc(s_selgo, 1)
                step(lambda: v.tensor_reduce(gsm[:, 0, 0:1], GATE[:, e], AX_X, ALU.add))
                step(lambda: v.reciprocal(gsm[:, 1, 0:1], gsm[:, 0, 0:1]))
                step(lambda: v.tensor_scalar(GATE[:, e], GATE[:, e], gsm[:, 1, 0:1], None, ALU.mult))
                assert state["j"] == NSEL

            def experts(layer):
                u0 = layer * UNITS
                norm(2 * layer + 1)
                v.wait_ge(s_crow, 32)
                hs = H[:, :, NP_TOK:TOK].unsqueeze(2).broadcast_to([P, DC, 4, NS_TOK])
                V.do(v.tensor_copy(HS4.rearrange("p c (g t) -> p c g t", g=4), hs), s_hs4)
                V.chain(v.memset(QP, 0.0))

                def v_indices(e):
                    v.tensor_scalar(CURV[:, e, :], IDX[:, e], float(layer * NEXP), None, ALU.add).then_inc(s_vidx, 1)

                def z_of(u, k, e, h):
                    v.wait_ge(u_land[k % RING], u * 32 + 16 * (k // RING + 1))
                    v.scalar_tensor_tensor(RU[:, k % RING, :], RU[:, k % RING, :], 1.0, h, ALU.mult, ALU.mult,
                                           accum_out=ZB[:, e, k:k + 1]).then_inc(s_z, 1)

                for _ in choose(u0, 0, layer):
                    pass
                for j in range(2):
                    n = GROUP[f"hf{layer}"] + j
                    v.wait_ge(bank_free[n % BANKS], n // BANKS + 1)
                for k in range(RING):
                    z_of(u0, k, 0, HTOK[:, 0, :])
                for _ in choose(u0 + 1, 1, layer):
                    pass
                for k in range(RING, TOPK):
                    z_of(u0, k, 0, HTOK[:, 0, :])
                v.wait_ge(s_sel, (u0 + 2) * NSEL)
                v_indices(0)
                v.wait_ge(s_q, 16 * (layer + 1))
                for g in range(4):
                    V.do(v.tensor_copy(QP[:, 4 * g:4 * g + 4, 32 * g:32 * g + 32], Q[:, 4 * g:4 * g + 4, NP_TOK:TOK]))
                V.sync()
                v.sem_inc(s_qp, 1)
                for j in range(4):
                    n = GROUP[f"ht{layer}"] + j
                    v.wait_ge(bank_free[n % BANKS], n // BANKS + 1)
                V.chain(v.memset(OACC, 0.0))

                def unit(u, lu, e, last):
                    chosen = choose(u + 2, e, layer) if last == 0 else iter(())
                    if last < 2:
                        for k in range(TOPK):
                            if k == 2:
                                coef(u, e)
                            if k == 8:
                                v.wait_ge(s_sel, u * NSEL + 2 * NSEL)
                                v.wait_ge(v_free, u * 16 + RING)
                                v_indices(1 - e)
                            z_of(u + 1, k, 1 - e, at(HTOK, (lu + 1) // 8))
                            if k >= 2:
                                next(chosen, None)
                    else:
                        coef(u, e)
                    for _ in chosen:
                        pass
                    v.wait_ge(v_free, u * 16 + (16 + RING))
                    v.wait_ge(acc_free, u + 2)
                    oa = at(OACC, lu // 8)
                    v.tensor_tensor(oa, oa, ps[:, 4 + 2 * e:6 + 2 * e, :].rearrange("p b n -> p (b n)"), ALU.add).then_inc(acc_free, 1)

                def coef(u, e):
                    v.wait_ge(s_sel, u * NSEL + NSEL)
                    v.wait_ge(s_gelu, u + 1)
                    v.tensor_tensor(CF[:, e, :], GL[:, e, :], GATE[:, e], ALU.mult).then_inc(s_coef, 1)

                with v.Fori(0, UNITS // 2 - 1) as i:
                    for e in range(2):
                        unit(i * 2 + (u0 + e), i * 2 + e, e, 0)
                for e in range(2):
                    unit(u0 + UNITS - 2 + e, UNITS - 2 + e, e, 1 + e)
                v.wait_ge(acc_free, u0 + UNITS + 2)
                v.sem_inc(s_acc, 1)
                residual(f"res{layer}", 2 * layer + 1)

            def by_chunk(f):
                return f[:, :, 0:NP_TOK].rearrange("p c (q t) -> p c q t", t=CHUNK)

            def rwkv():
                v.wait_ge(s_const, 2)
                V.do(v.tensor_copy(TOKM[NS_TOK:2 * NS_TOK], TOKM[0:NS_TOK]))
                sh = H[:, :, NP_TOK:TOK].rearrange("p c (b t) -> p c b t", b=NSEQ)
                sx = sample(XX)
                V.do(v.tensor_tensor(sx[:, :, :, 1:NSTEP], sh[:, :, :, 0:NSTEP - 1], sh[:, :, :, 1:NSTEP], ALU.subtract))
                V.do(v.tensor_tensor(sx[:, :, :, 0], CT[:, :, CR_SHIFT:CR_SHIFT + NSEQ], sh[:, :, :, 0], ALU.subtract))

                def mix(i, which, c):
                    return V.do(v.scalar_tensor_tensor((XI0, XI1)[i % 2][:, c, :], XX[:, c, :], col("rwkv_mix", 8 * which + c),
                                                       H[:, c, :], ALU.mult, ALU.add))

                for c in range(DC):
                    v.wait_ge(s_hp, 2 * DC + c + 1)
                    V.do(v.tensor_tensor(XX[:, c, 1:NP_TOK], H[:, c, 0:NP_TOK - 1], H[:, c, 1:NP_TOK], ALU.subtract))
                    V.do(v.tensor_scalar(XX[:, c, 0:1], H[:, c, 0:1], -1.0, None, ALU.mult))
                    V.sync()
                    mix(0, 0, c)
                    V.sync()
                    v.sem_inc(s_x0, 1)
                v.sem_inc(s_xi, 1)
                V.do(v.tensor_copy(COUT[:, :, 0:1], H[:, :, NP_TOK - 1:NP_TOK]))
                V.do(v.tensor_copy(COUT[:, :, 1:NCOND], sh[:, :, :, NSTEP - 1]))
                V.sync()
                v.sem_inc(s_sh, 1)
                for i, which in enumerate((0, 2, 3, 1, 4, 5)):
                    if i == 0:
                        continue
                    if i >= 2:
                        last = [GROUP["rp"] + DC, GROUP["kp"] + DC, GROUP["vp"] + DC, GROUP["lm"] + 1][i - 2]
                        v.wait_ge(bank_ready, last)
                    for c in range(DC):
                        mix(i, which, c)
                    V.sync()
                    v.sem_inc(s_xi, 1)
                V.do(v.tensor_scalar(OMKA[:], cols("rwkv_k_a", DC), -1.0, 1.0, ALU.mult, ALU.add))
                V.sync()
                v.wait_ge(s_sg, 1)
                v.wait_ge(s_shr, 32)
                for c in range(DC):
                    V.do(v.tensor_scalar(AF[:, c, :], KF[:, c, :], col("rwkv_k_k", c), None, ALU.mult))
                V.sync()
                v.sem_inc(s_kk, 1)
                for c in range(DC):
                    V.do(v.tensor_scalar(XX[:, c, :], BF[:, c, :], col("rwkv_k_a", c), OMKA[:, c:c + 1], ALU.mult, ALU.add))
                V.sync()
                V.chain(v.tensor_tensor(KF, KF, XX, ALU.mult))
                V.chain(v.tensor_scalar(LW, LW, DECAY, None, ALU.mult))
                for c in range(DC):
                    V.do(v.tensor_tensor_scan(XX[:, c, :], SCM[:], LW[:, c, :], 0.0, ALU.mult, ALU.add))
                V.sync()
                for c in range(DC):
                    o, free = take("kn", c)
                    V.do(v.tensor_scalar(XI0[:, c, :], o[:, 0:TOK], 1e-24, None, ALU.max))
                    free_bank(free)
                v.sem_inc(s_kkn, 1)
                for c in range(DC):
                    V.do(v.scalar_tensor_tensor(XI1[:, c, :], RF[:, c, :], col("rwkv_r_k", c), KF[:, c, :], ALU.mult, ALU.mult))
                V.sync()
                v.sem_inc(s_rk, 1)
                v.wait_ge(s_kkr, 1)
                V.chain(v.reciprocal(XI0, XI0))
                V.chain(v.tensor_tensor(AF, AF, XI0, ALU.mult))
                for c in range(DC):
                    o, free = take("bn", c)
                    V.do(v.tensor_tensor(BON[:, c, :], o[:, 0:TOK], VF[:, c, :], ALU.mult))
                    free_bank(free)
                V.chain(v.tensor_tensor(BF, BF, AF, ALU.mult))
                mid = CHUNK // 2 - 1
                cc = by_chunk(XX)
                V.do(v.tensor_tensor(by_chunk(XI0), cc, cc[:, :, :, mid:mid + 1].broadcast_to([P, DC, NQ, CHUNK]), ALU.subtract))
                V.do(v.tensor_copy(XI0[:, :, NP_TOK:TOK], XX[:, :, NP_TOK:TOK]))
                V.do(v.tensor_copy(EC[:], sample(XX)[:, :, :, NSTEP - 1]))
                V.chain(v.tensor_tensor(FE[:], cc[:, :, :, CHUNK - 1], cc[:, :, :, mid], ALU.subtract))
                V.do(v.tensor_tensor(FE[:, :, 0:NQ - 1], FE[:, :, 0:NQ - 1], cc[:, :, 1:NQ, mid], ALU.add))
                V.do(v.tensor_tensor(LW, XI0, LW, ALU.subtract))
                V.sync()
                v.sem_inc(s_dc, 1)
                v.wait_ge(s_ex, 3)
                V.chain(v.tensor_tensor(RF, RF, XI1, ALU.mult))
                v.sem_inc(s_exu, 1)
                v.wait_ge(s_ex, 4)
                V.do(v.tensor_tensor(KF, KF, XI1, ALU.mult))
                V.chain(v.tensor_tensor(BF, BF, XI1, ALU.mult))
                v.sem_inc(s_exu, 1)
                v.wait_ge(s_ex, 5)
                V.do(v.scalar_tensor_tensor(AF, AF, -1.0, LW, ALU.mult, ALU.mult))
                ecb = EC[:].unsqueeze(3).broadcast_to([P, DC, NSEQ, NSTEP])
                for i, f in enumerate((BF, KF)):
                    V.do(v.tensor_tensor(BBS[:, i].rearrange("p c (b t) -> p c b t", b=NSEQ), sample(f), ecb, ALU.mult))
                V.sync()
                v.sem_inc(s_wkv, 1)
                V.do(v.memset(SB, 0.0))
                V.do(v.memset(RAW, 0.0))
                V.sync()
                v.sem_inc(s_wkv, 1)
                v.sem_inc(s_raw0, 1)
                def group_norm(tile):
                    n = P if tile < 2 else NS_TOK
                    y3 = YR[0:n].rearrange("p (h i) -> p h i", h=WHEADS)
                    k3 = (SA.rearrange("p c i -> p (c i)") if tile < 2 else KTK)[0:n].rearrange("p (h i) -> p h i", h=WHEADS)
                    wide16 = lambda s: s.unsqueeze(2).broadcast_to([n, WHEADS, HS])
                    if tile < 2:
                        for j in (14, 15):
                            ny = GROUP[f"sq{tile}"] + j
                            v.wait_ge(bank_free[ny % BANKS], ny // BANKS + 1)
                    V.chain(v.tensor_reduce(gst[0:n, 0, :], y3, AX_X, ALU.add))
                    yield
                    V.chain(v.tensor_scalar(gst[0:n, 0, :], gst[0:n, 0, :], -1.0 / HS, None, ALU.mult))
                    yield
                    V.chain(v.tensor_tensor(y3, y3, wide16(gst[0:n, 0, :]), ALU.add))
                    yield
                    V.chain(v.tensor_tensor(k3, y3, y3, ALU.mult))
                    yield
                    V.chain(v.tensor_reduce(gst[0:n, 1, :], k3, AX_X, ALU.add))
                    yield
                    V.chain(v.tensor_scalar(gst[0:n, 1, :], gst[0:n, 1, :], 1.0 / HS, GN_EPS, ALU.mult, ALU.add), s_gn)
                    yield
                    if tile < 2:
                        for _ in range(4):
                            yield
                    v.wait_ge(s_gnr, tile + 1)
                    V.chain(v.reciprocal(gst[0:n, 2, :], gst[0:n, 1, :]))
                    yield
                    V.chain(v.tensor_tensor(y3, y3, wide16(gst[0:n, 2, :]), ALU.mult))
                    v.sem_inc(s_yn, 1)

                def normed_y(tile):
                    n = P if tile < 2 else NS_TOK
                    for q in range(2):
                        o, free = take(f"gn{tile}", q)
                        for j in range(4):
                            c = 4 * q + j
                            V.do(v.tensor_scalar(H[:, c, tile * P:tile * P + n], o[:, j * n:(j + 1) * n], col("rwkv_lnw", c),
                                                 col("rwkv_lnb", c), ALU.mult, ALU.add))
                        free_bank(free)

                def gated(t, c=slice(0, DC)):
                    V.chain(v.tensor_tensor(H[:, c, t], H[:, c, t], BON[:, c, t], ALU.add))
                    V.do(v.tensor_tensor(H[:, c, t], H[:, c, t], GF[:, c, t], ALU.mult))
                    V.sync()

                between = iter(())
                for tile in range(3):
                    n = P if tile < 2 else NS_TOK
                    nm = f"nm{tile}"
                    steps = NM_STEPS if tile < 2 else NM_STEPS_S

                    def wide(m):
                        return m[0:n].unsqueeze(1).broadcast_to([n, 4, n])

                    for bp in range(2):
                        for step in range(steps):
                            for b in range(2):
                                if step in ((5, 6, 9, 10, 13, 16, 19) if tile < 2 else (5,)):
                                    continue
                                o, free = take(nm + "ab"[bp], step * 2 + b)
                                o = o[0:n, 0:4 * n].rearrange("p (h t) -> p h t", h=4)
                                h0 = slot(2 * 4 * bp + b)
                                gg = [(GG[0:n, i] if tile < 2 else GS[i][0:n])[:, h0:h0 + 4, :] for i in range(4)]
                                T = NT[0:n, b, :, :, 0:n]
                                G = gg[3]
                                if step == 0:
                                    V.chain(v.tensor_tensor(T[:, 1], o, wide(M8U if tile < 2 else M4U), ALU.mult))
                                    V.chain(v.tensor_tensor(G, T[:, 1], wide(ident[:, 0:n]), ALU.add))
                                elif step == 1:
                                    V.do(v.tensor_tensor(T[:, 0], o, wide(M8A if tile < 2 else M4A), ALU.mult))
                                    if tile < 2:
                                        for i, m in enumerate((O8A, O16A, O32A)):
                                            V.do(v.tensor_tensor(T[:, 5 + i], o, wide(m), ALU.mult))
                                        V.sync()
                                        V.do(v.tensor_tensor(T[:, 4], T[:, 0], wide(ident[:]), ALU.add))
                                elif step < 5:
                                    mask = ((S64U, I64U, I64U) if tile < 2 else (M4U, I4U, I4U))[step - 2]
                                    V.do(v.tensor_tensor(gg[step - 2], o, wide(mask), ALU.mult))
                                else:
                                    dst = T[:, 4] if step in (8, 12, 15, 18) else G
                                    V.do(v.tensor_tensor(dst, dst, o, ALU.add))
                                free_bank(free)
                                next(between, None)
                        if tile > 0 and bp == 0:
                            for _ in between:
                                pass
                            normed_y(tile - 1)
                    if tile < 2:
                        for ch in range(2):
                            for q in range(2):
                                o, free = take(f"sq{tile}", 8 * ch + 4 + q)
                                for j in range(4):
                                    c = 4 * q + j
                                    V.do(v.scalar_tensor_tensor(state_of(2 * tile + ch + 1, c), o[:, j * P:(j + 1) * P], FE[:, c, 2 * tile + ch:2 * tile + ch + 1],
                                                                BLK, ALU.mult, ALU.mult))
                                free_bank(free)
                        between = group_norm(tile)
                    else:
                        tok = TOKM[0:2 * n].unsqueeze(2).broadcast_to([2 * n, NSEQ, P])

                        def masked(c):
                            for i, f in enumerate((AF, RF)):
                                V.do(v.tensor_tensor(ART[:, c % 2, :, i, :], f[:, c, NP_TOK:TOK].unsqueeze(1).broadcast_to([P, NSEQ, NS_TOK]),
                                                     SEQM[:], ALU.mult))
                            V.sync()
                            v.sem_inc(s_atm, 1)

                        v.wait_ge(s_v2, 1)
                        for c in range(2):
                            masked(c)
                        gains("ad7", (3,))
                        for kind, c in SQ2:
                            if kind[:4] in ("turn", "out0", "out1"):
                                continue
                            o, free = take("sq2", SQ2.index((kind, c)))
                            pair = slice(c * P, (c + 1) * P)
                            if kind == "right":
                                V.do(v.tensor_copy(RHS[0:n], o[0:n, 0:P]))
                                V.do(v.tensor_copy(YR[0:n, pair], o[n:2 * n, 0:P]))
                                free_bank(free)
                                if 0 < c < DC - 1:
                                    masked(c + 1)
                            elif kind == "sa":
                                V.do(v.tensor_copy(SAV[0:n, pair], o[0:n, 0:P]))
                                free_bank(free)
                                V.chain(v.tensor_tensor(SAVM[0:2 * n], SAV[0:2 * n, pair].unsqueeze(1).broadcast_to([2 * n, NSEQ, P]),
                                                        tok, ALU.mult))
                                v.sem_inc(s_sam, 1)
                                for k in ("turn0", "turn1"):
                                    nt = GROUP["sq2"] + SQ2.index((k, c))
                                    v.wait_ge(bank_free[nt % BANKS], nt // BANKS + 1)
                                V.chain(v.tensor_tensor(NEW[:, c % 2], SS[:, c % 2], EC[:, c, :].unsqueeze(2).broadcast_to([P, NSEQ, P]),
                                                        ALU.mult))
                                v.sem_inc(s_kept, 1)
                                gated(slice(0, NP_TOK), slice(c, c + 1))
                            elif kind == "y":
                                V.do(v.tensor_tensor(YR[0:n, pair], YR[0:n, pair], o[0:n, 0:P], ALU.add))
                                free_bank(free)
                            else:
                                half = int(kind[-1])
                                dst = NEW[:, c % 2, 4 * half:4 * half + 4, :]
                                V.do(v.tensor_tensor(dst, dst, o.rearrange("p (s n) -> p s n", s=4), ALU.add))
                                free_bank(free)
                for _ in group_norm(2):
                    pass
                normed_y(2)
                gated(slice(NP_TOK, TOK))
                v.sem_inc(s_wy, 1)
                residual("wo", 2)

            experts(0)
            norm(2)
            rwkv()
            v.wait_ge(s_stout[0], 16 * DC)
            v.wait_ge(s_stout[1], 16 * DC)
            experts(1)
            norm(4)

        @block.gpsimd
        def _(pool):
            G = Steps(pool, pool_step)
            G.chain(pool.memset(ident[:], 0.0))
            G.chain(pool.affine_select(out=ident[:], in_=ident[:], compare_op=ALU.not_equal, fill=1.0, base=0,
                                       pattern=[[-1, P]], channel_multiplier=1))
            G.do(pool.memset(ones[:], 1.0))
            G.do(pool.iota(iota16[:], pattern=[[1, TOPK]], base=0, channel_multiplier=0, allow_small_or_imprecise_dtypes=True))
            def mask(dst, n, block, tri, inner=None):
                def keep(v, pattern, base, mult, op=ALU.is_ge):
                    G.chain(pool.affine_select(out=v, in_=v, compare_op=op, fill=0.0, base=base, pattern=pattern,
                                               channel_multiplier=mult))

                G.chain(pool.memset(dst, 1.0))
                v3 = dst.rearrange("p (b r) -> p b r", r=block)
                keep(v3, [[-block, n // block], [0, block]], 0, 1)
                keep(v3, [[block, n // block], [0, block]], block - 1, -1)
                if tri in ("u", "U"):
                    keep(dst, [[1, n]], -1 if tri == "u" else 0, -1)
                elif tri == "l":
                    keep(dst, [[-1, n]], -1, 1)
                if inner:
                    keep(dst.rearrange("p (b r) -> p b r", r=inner), [[-inner, n // inner], [0, inner]], -inner, 1)

            G.sync()
            pool.sem_inc(s_const, 1)
            mask(M8U, P, 8, "u")
            mask(M8A, P, 8, "l")
            mask(O8A, P, 16, "l", 8)
            mask(O16A, P, 32, "l", 16)
            mask(O32A, P, 64, "l", 32)
            mask(S64U, P, CHUNK, "u")
            mask(I64U, P, CHUNK, "U")
            mask(BLK, P, HS, None)
            mask(M4U, NS_TOK, NSTEP, "u")
            mask(M4A, NS_TOK, NSTEP, "l")
            mask(I4U, NS_TOK, NSTEP, "U")
            G.chain(pool.memset(SEQM[:], 1.0))
            for base, mult in ((0, 1), (NSTEP - 1, -1)):
                G.chain(pool.affine_select(out=SEQM[:], in_=SEQM[:], compare_op=ALU.is_ge, fill=0.0, base=base,
                                           pattern=[[-NSTEP * mult, NSEQ], [mult, NS_TOK]], channel_multiplier=0))
            G.chain(pool.memset(TOKM[:], 1.0))
            for base, mult in ((0, 1), (NSTEP - 1, -1)):
                G.chain(pool.affine_select(out=TOKM[:], in_=TOKM[:], compare_op=ALU.is_ge, fill=0.0, base=base,
                                           pattern=[[-NSTEP * mult, NSEQ]], channel_multiplier=mult))
            G.chain(pool.memset(SCM[:], 1.0))
            G.do(pool.memset(SCM[:, 0:NP_TOK].rearrange("p (q t) -> p q t", t=CHUNK)[:, :, 0:1], 0.0))
            G.do(pool.memset(SCM[:, NP_TOK:].rearrange("p (q t) -> p q t", t=NSTEP)[:, :, 0:1], 0.0))
            G.sync()
            pool.sem_inc(s_const, 1)
            u_tab = a["peer_u"].rearrange("l e d -> (l e) d")
            v_tab = a["peer_v"].rearrange("l e d -> (l e) d")

            def gather(ring, tab, idx, k, landed):
                pool.indirect_dma_start(ring[:, k % RING, :], None, tab,
                                        bass.IndirectOffsetOnAxis(ap=idx[:, k:k + 1], axis=0)).then_inc(landed[k % RING], 16)

            def experts(layer):
                u0 = layer * UNITS

                def get_u(u, k, e):
                    if k == 0:
                        pool.wait_ge(s_sel, u * NSEL + SEL_IDX)
                    if k >= RING or not isinstance(u, int) or u > 0:
                        pool.wait_ge(s_z, u * 16 + (k - RING + 1))
                    pool.sem_inc(s_go, 1)
                    gather(RU, u_tab, CURU[:, e, :], k, u_land)

                def get_v(u, k, e):
                    if k == 0:
                        pool.wait_ge(s_vidx, u + 1)
                    pool.wait_ge(v_free, u * 16 + (k + 1))
                    pool.sem_inc(s_go, 1)
                    gather(RVV, v_tab, CURV[:, e, :], k, v_land)

                for k in range(TOPK):
                    get_u(u0, k, 0)
                for k in range(RING):
                    get_u(u0 + 1, k, 1)
                pool.wait_ge(bank_ready, GROUP[f"sc{layer}"] + 9)
                for e in range(2):
                    for k in range(TOPK):
                        get_v(u0 + e, k, e)
                        if e == 1 or k >= RING:
                            get_u(u0 + e + 1, k, 1 - e)
                with pool.Fori(0, UNITS // 2 - 2) as i:
                    for e in range(2):
                        for k in range(TOPK):
                            get_v(i * 2 + (u0 + 2 + e), k, e)
                            get_u(i * 2 + (u0 + 2 + e + 1), k, 1 - e)
                for k in range(TOPK):
                    get_v(u0 + UNITS - 2, k, 0)
                    get_u(u0 + UNITS - 1, k, 1)
                for k in range(TOPK):
                    get_v(u0 + UNITS - 1, k, 1)

            experts(0)
            experts(1)


_INS = ['x_prompt', 'x_sample', 'state_conv', 'state_shift', 'state_wkv', 'c_prompt', 'c_sample', 'w_ada', 'b_ada',
        'g_mix', 'g_ffn', 'g_final', 'conv_w_in', 'conv_k', 'conv_w_out', 'rwkv_mix', 'rwkv_wr', 'rwkv_wk', 'rwkv_wv',
        'rwkv_wo', 'rwkv_w0', 'rwkv_w1', 'rwkv_w2', 'rwkv_a0', 'rwkv_a1', 'rwkv_a2', 'rwkv_g1', 'rwkv_g2', 'rwkv_k_k',
        'rwkv_k_a', 'rwkv_r_k', 'rwkv_lnw', 'rwkv_lnb', 'peer_wq', 'peer_k1', 'peer_k2', 'peer_u', 'peer_v']
_OUTS = [(1, 256, 1024), (8, 4, 1024), (1, 1, 2, 1024), (1, 1, 1024), (1, 1, 16, 64, 64), (1, 8, 2, 1024),
         (1, 8, 1024), (1, 8, 16, 64, 64)]


def kernel(**inputs):
    import numpy as _np
    import concourse.bacc as _bacc
    from concourse import mybir as _mybir
    from concourse.bass_utils import run_bass_kernel_spmd as _run

    nc = _bacc.Bacc("TRN2", target_bir_lowering=False, num_devices=1)
    arrays, aps, outs = {}, {}, []
    for name in _INS:
        x = _np.ascontiguousarray(inputs[name])
        arrays[f"in_{name}"] = x
        aps[name] = nc.dram_tensor(f"in_{name}", x.shape, _mybir.dt.from_np(x.dtype), kind="ExternalInput").ap()
    for i, shape in enumerate(_OUTS):
        outs.append(nc.dram_tensor(f"out_{i}", shape, _mybir.dt.float32, kind="ExternalOutput").ap())
    build(nc, aps, outs)
    r = _run(nc, [arrays], core_ids=[0])
    return tuple(r.results[0][f"out_{i}"] for i in range(len(_OUTS)))
```
